# Optimizing a Trainium2 kernel written in Bass

```python
import math
import jax, jax.numpy as jnp
from jax import lax
import numpy as np
import jax
import jax.numpy as jnp

D_MODEL = 2048
BATCH = 1
SEQ = 256
DEPTH = 1

HEAD_DIM = 64
N_Q_HEADS = 16
N_KV_HEADS = 4
Q_PER_KV = N_Q_HEADS // N_KV_HEADS
ATTN_WIDTH = N_Q_HEADS * HEAD_DIM
KV_WIDTH = N_KV_HEADS * HEAD_DIM
WINDOW = 128
BLOCK = 128
SSM_WIDTH = D_MODEL - ATTN_WIDTH
SSM_GROUP = 16
SSM_GROUPS = SSM_WIDTH // SSM_GROUP
SSM_STATE = 64
MIX_WIDTH = ATTN_WIDTH + SSM_WIDTH
IN_WIDTH = ATTN_WIDTH + 2 * KV_WIDTH + SSM_WIDTH
FF_HIDDEN = -(-8 * D_MODEL // (3 * 256)) * 256
REL_BUCKETS = 32
REL_MAX_DISTANCE = 128
EPS = 1e-6


def _rmsnorm(x, g):
    xf = x.astype(jnp.float32)
    y = xf * lax.rsqrt(jnp.mean(xf * xf, axis=-1, keepdims=True) + EPS)
    return (y * g.astype(jnp.float32)).astype(x.dtype)

def _t5_bucket(dist):
    n = np.maximum(dist, 0)
    max_exact = REL_BUCKETS // 2
    nf = np.maximum(n, 1).astype(np.float32)
    large = max_exact + (np.log(nf / max_exact) / math.log(REL_MAX_DISTANCE / max_exact)
                         * (REL_BUCKETS - max_exact)).astype(np.int32)
    large = np.minimum(large, REL_BUCKETS - 1)
    return np.where(n < max_exact, n, large).astype(np.int32)

def _sliding_window_attention(q, k, v, sinks, rel_bias):
    bsz, L = q.shape[0], q.shape[1]
    nb = L // BLOCK
    qb = q.reshape(bsz, nb, BLOCK, N_KV_HEADS, Q_PER_KV, HEAD_DIM)
    pad = ((0, 0), (BLOCK, 0), (0, 0), (0, 0))
    kp = jnp.pad(k, pad).reshape(bsz, nb + 1, BLOCK, N_KV_HEADS, HEAD_DIM)
    vp = jnp.pad(v, pad).reshape(bsz, nb + 1, BLOCK, N_KV_HEADS, HEAD_DIM)
    kb = jnp.concatenate([kp[:, :-1], kp[:, 1:]], axis=2)
    vb = jnp.concatenate([vp[:, :-1], vp[:, 1:]], axis=2)
    logits = jnp.einsum('bnqkgd,bnskd->bnkgqs', qb, kb).astype(jnp.float32) * (HEAD_DIM ** -0.5)

    qi = np.arange(BLOCK)[:, None]
    sj = np.arange(2 * BLOCK)[None, :]
    dist = qi + BLOCK - sj
    bucket = _t5_bucket(dist)
    bias = jnp.transpose(rel_bias[bucket].astype(jnp.float32), (2, 0, 1))
    bias = bias.reshape(N_KV_HEADS, Q_PER_KV, BLOCK, 2 * BLOCK)
    in_window = (dist >= 0) & (dist < WINDOW)
    key_pos = np.arange(nb)[:, None] * BLOCK - BLOCK + np.arange(2 * BLOCK)[None, :]
    valid = in_window[None] & (key_pos >= 0)[:, None, :]
    logits = jnp.where(valid[None, :, None, None], logits + bias, -jnp.inf)

    sink = sinks.astype(jnp.float32).reshape(N_KV_HEADS, Q_PER_KV, 1, 1)
    m = jnp.maximum(jnp.max(logits, axis=-1, keepdims=True), sink)
    p = jnp.exp(logits - m)
    w = p / (jnp.sum(p, axis=-1, keepdims=True) + jnp.exp(sink - m))
    out = jnp.einsum('bnkgqs,bnskd->bnqkgd', w.astype(v.dtype), vb)
    return out.reshape(bsz, L, ATTN_WIDTH)

def _scan_combine(a, b):
    a_re, a_im, x_re, x_im = a
    b_re, b_im, y_re, y_im = b
    n_re = b_re * a_re - b_im * a_im
    n_im = b_re * a_im + b_im * a_re
    o_re = b_re * x_re - b_im * x_im + y_re
    o_im = b_re * x_im + b_im * x_re + y_im
    return (n_re, n_im, o_re, o_im)

def _s5_mixer(u, a_re, a_im, log_dt, b_re, b_im, c_re, c_im, d, w_glu):
    bsz, L = u.shape[0], u.shape[1]
    f32 = jnp.float32
    uf = u.reshape(bsz, L, SSM_GROUPS, SSM_GROUP).astype(f32)
    a_re = a_re.astype(f32)
    a_im = a_im.astype(f32)
    dt = jnp.exp(log_dt.astype(f32))[:, None]
    mag = jnp.exp(a_re * dt)
    ang = a_im * dt
    lb_re, lb_im = mag * jnp.cos(ang), mag * jnp.sin(ang)
    nr, ni = lb_re - 1.0, lb_im
    den = a_re * a_re + a_im * a_im
    f_re = (nr * a_re + ni * a_im) / den
    f_im = (ni * a_re - nr * a_im) / den
    b_re = b_re.astype(f32)
    b_im = b_im.astype(f32)
    bb_re = f_re[..., None] * b_re - f_im[..., None] * b_im
    bb_im = f_re[..., None] * b_im + f_im[..., None] * b_re
    bu_re = jnp.einsum('blgp,gnp->blgn', uf, bb_re)
    bu_im = jnp.einsum('blgp,gnp->blgn', uf, bb_im)
    shape_a = (1, L, SSM_GROUPS, SSM_STATE)
    elems = (jnp.broadcast_to(lb_re, shape_a), jnp.broadcast_to(lb_im, shape_a), bu_re, bu_im)
    _, _, h_re, h_im = lax.associative_scan(_scan_combine, elems, axis=1)
    y = (jnp.einsum('blgn,gpn->blgp', h_re, c_re.astype(f32))
         - jnp.einsum('blgn,gpn->blgp', h_im, c_im.astype(f32))
         + d.astype(f32) * uf)
    y = jax.nn.gelu(y.reshape(bsz, L, SSM_WIDTH)).astype(u.dtype)
    return y * jax.nn.sigmoid(y @ w_glu)

def _layer(x, rel_bias, ln1_g, w_in, q_norm_g, k_norm_g, attn_sinks, ssm_a_re, ssm_a_im,
           ssm_log_dt, ssm_b_re, ssm_b_im, ssm_c_re, ssm_c_im, ssm_d, w_glu,
           attn_out_g, ssm_out_g, w_out, ln2_g, w_ff_gate, w_ff_up, w_ff_down):
    bsz, L = x.shape[0], x.shape[1]
    h = _rmsnorm(x, ln1_g)
    proj = h @ w_in
    q, k, v, u = jnp.split(proj, [ATTN_WIDTH, ATTN_WIDTH + KV_WIDTH, ATTN_WIDTH + 2 * KV_WIDTH], axis=-1)
    q = _rmsnorm(q.reshape(bsz, L, N_Q_HEADS, HEAD_DIM), q_norm_g)
    k = _rmsnorm(k.reshape(bsz, L, N_KV_HEADS, HEAD_DIM), k_norm_g)
    v = v.reshape(bsz, L, N_KV_HEADS, HEAD_DIM)
    y_attn = _sliding_window_attention(q, k, v, attn_sinks, rel_bias)
    y_ssm = _s5_mixer(u, ssm_a_re, ssm_a_im, ssm_log_dt, ssm_b_re, ssm_b_im,
                      ssm_c_re, ssm_c_im, ssm_d, w_glu)
    mixed = jnp.concatenate([_rmsnorm(y_attn, attn_out_g), _rmsnorm(y_ssm, ssm_out_g)], axis=-1)
    x = x + mixed @ w_out
    h2 = _rmsnorm(x, ln2_g)
    ff = (jax.nn.silu(h2 @ w_ff_gate) * (h2 @ w_ff_up)) @ w_ff_down
    return x + ff

def first_inputs(seed: int = 0) -> dict:
    key = jax.random.key(seed)
    ks = jax.random.split(key, 24)
    f32 = jnp.float32
    nrm = lambda k, s, sc: jax.random.normal(k, s, f32) * sc
    Dp = DEPTH
    n_idx = jnp.arange(SSM_STATE, dtype=f32)
    return {
        "x": nrm(ks[0], (BATCH, SEQ, D_MODEL), 1.0),
        "rel_bias": nrm(ks[1], (REL_BUCKETS, N_Q_HEADS), 0.5),
        "ln1_g": 1.0 + nrm(ks[2], (Dp, D_MODEL), 0.02),
        "w_in": nrm(ks[3], (Dp, D_MODEL, IN_WIDTH), D_MODEL ** -0.5),
        "q_norm_g": 1.0 + nrm(ks[4], (Dp, HEAD_DIM), 0.02),
        "k_norm_g": 1.0 + nrm(ks[5], (Dp, HEAD_DIM), 0.02),
        "attn_sinks": nrm(ks[6], (Dp, N_Q_HEADS), 0.5),
        "ssm_a_re": -0.5 + nrm(ks[7], (Dp, SSM_GROUPS, SSM_STATE), 0.01),
        "ssm_a_im": math.pi * n_idx + nrm(ks[8], (Dp, SSM_GROUPS, SSM_STATE), 0.01),
        "ssm_log_dt": jax.random.uniform(ks[9], (Dp, SSM_GROUPS), f32, math.log(1e-3), math.log(1e-1)),
        "ssm_b_re": nrm(ks[10], (Dp, SSM_GROUPS, SSM_STATE, SSM_GROUP), (2 * SSM_GROUP) ** -0.5),
        "ssm_b_im": nrm(ks[11], (Dp, SSM_GROUPS, SSM_STATE, SSM_GROUP), (2 * SSM_GROUP) ** -0.5),
        "ssm_c_re": nrm(ks[12], (Dp, SSM_GROUPS, SSM_GROUP, SSM_STATE), (2 * SSM_STATE) ** -0.5),
        "ssm_c_im": nrm(ks[13], (Dp, SSM_GROUPS, SSM_GROUP, SSM_STATE), (2 * SSM_STATE) ** -0.5),
        "ssm_d": nrm(ks[14], (Dp, SSM_GROUPS, SSM_GROUP), 1.0),
        "w_glu": nrm(ks[15], (Dp, SSM_WIDTH, SSM_WIDTH), SSM_WIDTH ** -0.5),
        "attn_out_g": 1.0 + nrm(ks[16], (Dp, ATTN_WIDTH), 0.02),
        "ssm_out_g": 1.0 + nrm(ks[17], (Dp, SSM_WIDTH), 0.02),
        "w_out": nrm(ks[18], (Dp, MIX_WIDTH, D_MODEL), MIX_WIDTH ** -0.5),
        "ln2_g": 1.0 + nrm(ks[19], (Dp, D_MODEL), 0.02),
        "w_ff_gate": nrm(ks[20], (Dp, D_MODEL, FF_HIDDEN), D_MODEL ** -0.5),
        "w_ff_up": nrm(ks[21], (Dp, D_MODEL, FF_HIDDEN), D_MODEL ** -0.5),
        "w_ff_down": nrm(ks[22], (Dp, FF_HIDDEN, D_MODEL), FF_HIDDEN ** -0.5),
    }

def first_block(x, rel_bias, ln1_g, w_in, q_norm_g, k_norm_g, attn_sinks, ssm_a_re, ssm_a_im,
              ssm_log_dt, ssm_b_re, ssm_b_im, ssm_c_re, ssm_c_im, ssm_d, w_glu,
              attn_out_g, ssm_out_g, w_out, ln2_g, w_ff_gate, w_ff_up, w_ff_down):
    for l in range(DEPTH):
        x = _layer(x, rel_bias, ln1_g[l], w_in[l], q_norm_g[l], k_norm_g[l], attn_sinks[l],
                   ssm_a_re[l], ssm_a_im[l], ssm_log_dt[l], ssm_b_re[l], ssm_b_im[l],
                   ssm_c_re[l], ssm_c_im[l], ssm_d[l], w_glu[l], attn_out_g[l], ssm_out_g[l],
                   w_out[l], ln2_g[l], w_ff_gate[l], w_ff_up[l], w_ff_down[l])
    return x


_first_inputs = first_inputs


def first_inputs(seed=0):
    import zlib

    import numpy as np

    out = dict(_first_inputs(seed))
    spreads = {}
    factors = {}
    for name, (base, spread) in spreads.items():
        noise = np.random.default_rng([zlib.crc32(name.encode()), seed]).standard_normal(out[name].shape)
        drawn = base * np.exp(spread * noise) if base else spread * noise
        out[name] = __import__('jax').numpy.asarray(drawn.astype(out[name].dtype))
    for name, factor in factors.items():
        out[name] = (out[name] * factor).astype(out[name].dtype)
    return out


_narrow_inputs = first_inputs


def first_inputs(seed=0):

    out = dict(_narrow_inputs(seed))
    wider = {'q_norm_g': 6.69,
     'k_norm_g': 5.68,
     'attn_sinks': 5.65,
     'ssm_a_re': 12.0,
     'attn_out_g': 5.94,
     'ssm_out_g': 6.12,
     'ln2_g': 5.87}
    for name, times in wider.items():
        mean = out[name].mean()
        out[name] = (mean + times * (out[name] - mean)).astype(out[name].dtype)
    return out


DEPTH_2 = 2

A_WIDTH = D_MODEL // 2
B_WIDTH = D_MODEL - A_WIDTH
A_GROUPS = 8
A_GROUP_DIM = A_WIDTH // A_GROUPS
CHUNK = 128
CONV_WIDTH = 3
ATTN_HEAD_DIM = 128
ATTN_HEADS = D_MODEL // ATTN_HEAD_DIM
DILATED_BRANCHES = ((128, 1), (512, 4), (2048, 16))
ATTN_BLOCK = 128
ROPE_THETA = 10000.0
FFN_DIM = 4 * D_MODEL
N_EVEN = (DEPTH_2 + 1) // 2
N_ODD = DEPTH_2 // 2
RMS_EPS = 1e-6
LN_EPS = 1e-5


def rmsnorm(x, g):
    xf = x.astype(jnp.float32)
    y = xf * lax.rsqrt(jnp.mean(xf * xf, axis=-1, keepdims=True) + RMS_EPS)
    return (y * g.astype(jnp.float32)).astype(x.dtype)

def rope(t, positions):
    dh = t.shape[-1]
    half = dh // 2
    inv_freq = ROPE_THETA ** (-jnp.arange(half, dtype=jnp.float32) * 2.0 / dh)
    ang = positions.astype(jnp.float32)[:, None] * inv_freq[None, :]
    cos = jnp.cos(ang)[None, :, None, :]
    sin = jnp.sin(ang)[None, :, None, :]
    t1 = t[..., :half].astype(jnp.float32)
    t2 = t[..., half:].astype(jnp.float32)
    out = jnp.concatenate([t1 * cos - t2 * sin, t2 * cos + t1 * sin], axis=-1)
    return out.astype(t.dtype)

def gmlp_shortconv_mixer(h, w_in, w_s, b_s, conv_w, w_out):
    bsz, s, _ = h.shape
    proj = h @ w_in
    a_u, a_v, g_b, g_c, b_x = jnp.split(
        proj, [A_WIDTH, 2 * A_WIDTH, 2 * A_WIDTH + B_WIDTH, 2 * A_WIDTH + 2 * B_WIDTH], axis=-1)

    a_u = jax.nn.gelu(a_u)
    a_v = jax.nn.gelu(a_v)
    vf = a_v.astype(jnp.float32)
    mu = jnp.mean(vf, axis=-1, keepdims=True)
    var = jnp.mean(jnp.square(vf - mu), axis=-1, keepdims=True)
    vn = ((vf - mu) * lax.rsqrt(var + LN_EPS)).astype(h.dtype)
    n_chunks = s // CHUNK
    vn = vn.reshape(bsz, n_chunks, CHUNK, A_GROUPS, A_GROUP_DIM)
    causal = jnp.tril(jnp.ones((CHUNK, CHUNK), dtype=bool))
    w_causal = jnp.where(causal[None], w_s, 0)
    mixed = jnp.einsum('gts,bnsgc->bntgc', w_causal, vn) + b_s.T[None, None, :, :, None]
    a_out = a_u * mixed.reshape(bsz, s, A_WIDTH)

    z = g_c * b_x
    zp = jnp.pad(z, ((0, 0), (CONV_WIDTH - 1, 0), (0, 0)))
    y = conv_w[0] * zp[:, 0:s]
    for tap in range(1, CONV_WIDTH):
        y = y + conv_w[tap] * zp[:, tap:tap + s]
    b_out = g_b * y

    return jnp.concatenate([a_out, b_out], axis=-1) @ w_out

def dilated_branch(q, k, v, window, dilation):
    bsz, s, nh, dh = q.shape
    n_steps = window // dilation
    blk = ATTN_BLOCK
    L = s // dilation
    nb = -(-L // blk)
    Lp = nb * blk

    def to_blocks(t):
        t = t.reshape(bsz, L, dilation, nh, dh).transpose(0, 2, 3, 1, 4)
        t = jnp.pad(t, ((0, 0), (0, 0), (0, 0), (0, Lp - L), (0, 0)))
        return t.reshape(bsz, dilation, nh, nb, blk, dh)

    def with_prev_block(t):
        prev = jnp.pad(t, ((0, 0), (0, 0), (0, 0), (1, 0), (0, 0), (0, 0)))[:, :, :, :-1]
        return jnp.concatenate([prev, t], axis=4)

    qb = to_blocks(q)
    kk = with_prev_block(to_blocks(k))
    vv = with_prev_block(to_blocks(v))

    scores = jnp.einsum('brhnqc,brhnkc->brhnqk', qb, kk).astype(jnp.float32) * (dh ** -0.5)
    qi = jnp.arange(blk)[:, None]
    ki = jnp.arange(2 * blk)[None, :]
    step = qi + blk - ki
    band = (step >= 0) & (step <= n_steps)
    key_idx = jnp.arange(nb)[:, None, None] * blk - blk + ki[None]
    mask = band[None] & (key_idx >= 0)
    scores = jnp.where(mask, scores, -jnp.inf)
    m = jnp.max(scores, axis=-1, keepdims=True)
    p = jnp.exp(scores - m)
    denom = jnp.sum(p, axis=-1, keepdims=True)
    o = jnp.einsum('brhnqk,brhnkc->brhnqc', (p / denom).astype(v.dtype), vv)
    lse = (m + jnp.log(denom))[..., 0]

    o = o.reshape(bsz, dilation, nh, Lp, dh)[:, :, :, :L].transpose(0, 3, 1, 2, 4).reshape(bsz, s, nh, dh)
    lse = lse.reshape(bsz, dilation, nh, Lp)[..., :L].transpose(0, 3, 1, 2).reshape(bsz, s, nh)
    return o, lse

def dilated_attention_mixer(h, w_qkv, w_o, positions):
    bsz, s, _ = h.shape
    qkv = h @ w_qkv
    q, k, v = jnp.split(qkv, 3, axis=-1)
    q = rope(q.reshape(bsz, s, ATTN_HEADS, ATTN_HEAD_DIM), positions)
    k = rope(k.reshape(bsz, s, ATTN_HEADS, ATTN_HEAD_DIM), positions)
    v = v.reshape(bsz, s, ATTN_HEADS, ATTN_HEAD_DIM)
    outs = []
    lses = []
    for window, dilation in DILATED_BRANCHES:
        o_i, lse_i = dilated_branch(q, k, v, window, dilation)
        outs.append(o_i.astype(jnp.float32))
        lses.append(lse_i)
    alpha = jax.nn.softmax(jnp.stack(lses, axis=0), axis=0)
    o = jnp.einsum('ibsh,ibshc->bshc', alpha, jnp.stack(outs, axis=0))
    return o.astype(h.dtype).reshape(bsz, s, ATTN_HEADS * ATTN_HEAD_DIM) @ w_o

def squared_relu_mlp(h, w_up, w_down):
    return jnp.square(jax.nn.relu(h @ w_up)) @ w_down

def second_inputs(seed: int = 0) -> dict:
    key = jax.random.key(seed)
    ks = jax.random.split(key, 14)
    f32 = jnp.float32
    d = D_MODEL
    x = jax.random.normal(ks[0], (BATCH, SEQ, d), f32)
    norm_mix_pre = 1.0 + 0.05 * jax.random.normal(ks[1], (DEPTH_2, d), f32)
    norm_mix_post = 1.0 + 0.05 * jax.random.normal(ks[2], (DEPTH_2, d), f32)
    norm_mlp_pre = 1.0 + 0.05 * jax.random.normal(ks[3], (DEPTH_2, d), f32)
    norm_mlp_post = 1.0 + 0.05 * jax.random.normal(ks[4], (DEPTH_2, d), f32)
    in_cols = 2 * A_WIDTH + 3 * B_WIDTH
    w_in_ab = jax.random.normal(ks[5], (N_EVEN, d, in_cols), f32) * d ** -0.5
    w_spatial = jax.random.normal(ks[6], (N_EVEN, A_GROUPS, CHUNK, CHUNK), f32) * (0.5 * CHUNK ** -0.5)
    b_spatial = 1.0 + 0.1 * jax.random.normal(ks[7], (N_EVEN, A_GROUPS, CHUNK), f32)
    conv_w = jax.random.normal(ks[8], (N_EVEN, CONV_WIDTH, B_WIDTH), f32) * CONV_WIDTH ** -0.5
    w_out_ab = jax.random.normal(ks[9], (N_EVEN, A_WIDTH + B_WIDTH, d), f32) * (A_WIDTH + B_WIDTH) ** -0.5
    attn_width = ATTN_HEADS * ATTN_HEAD_DIM
    w_qkv = jax.random.normal(ks[10], (N_ODD, d, 3 * attn_width), f32) * d ** -0.5
    w_o = jax.random.normal(ks[11], (N_ODD, attn_width, d), f32) * attn_width ** -0.5
    w_up = jax.random.normal(ks[12], (DEPTH_2, d, FFN_DIM), f32) * d ** -0.5
    w_down = jax.random.normal(ks[13], (DEPTH_2, FFN_DIM, d), f32) * FFN_DIM ** -0.5
    return {'x': x, 'norm_mix_pre': norm_mix_pre, 'norm_mix_post': norm_mix_post,
            'norm_mlp_pre': norm_mlp_pre, 'norm_mlp_post': norm_mlp_post,
            'w_in_ab': w_in_ab, 'w_spatial': w_spatial, 'b_spatial': b_spatial,
            'conv_w': conv_w, 'w_out_ab': w_out_ab, 'w_qkv': w_qkv, 'w_o': w_o,
            'w_up': w_up, 'w_down': w_down}

def second_block(x, norm_mix_pre, norm_mix_post, norm_mlp_pre, norm_mlp_post,
              w_in_ab, w_spatial, b_spatial, conv_w, w_out_ab, w_qkv, w_o,
              w_up, w_down):
    positions = jnp.arange(x.shape[1], dtype=jnp.int32)
    h = x
    for layer in range(DEPTH_2):
        hn = rmsnorm(h, norm_mix_pre[layer])
        if layer % 2 == 0:
            e = layer // 2
            mix = gmlp_shortconv_mixer(hn, w_in_ab[e], w_spatial[e], b_spatial[e], conv_w[e], w_out_ab[e])
        else:
            o = layer // 2
            mix = dilated_attention_mixer(hn, w_qkv[o], w_o[o], positions)
        h = h + rmsnorm(mix, norm_mix_post[layer])
        f = squared_relu_mlp(rmsnorm(h, norm_mlp_pre[layer]), w_up[layer], w_down[layer])
        h = h + rmsnorm(f, norm_mlp_post[layer])
    return h


def setup_inputs(seed=0):
    out = dict(first_inputs(seed))
    for name, value in second_inputs(seed + 1).items():
        if name != "x":
            out[name + "_2"] = value
    return out


def reference(
    x, rel_bias, ln1_g, w_in, q_norm_g, k_norm_g, attn_sinks, ssm_a_re, ssm_a_im, ssm_log_dt,
    ssm_b_re, ssm_b_im, ssm_c_re, ssm_c_im, ssm_d, w_glu, attn_out_g, ssm_out_g, w_out, ln2_g,
    w_ff_gate, w_ff_up, w_ff_down, norm_mix_pre_2, norm_mix_post_2, norm_mlp_pre_2,
    norm_mlp_post_2, w_in_ab_2, w_spatial_2, b_spatial_2, conv_w_2, w_out_ab_2, w_qkv_2, w_o_2,
    w_up_2, w_down_2,
):
    x = first_block(
        x, rel_bias, ln1_g, w_in, q_norm_g, k_norm_g, attn_sinks, ssm_a_re, ssm_a_im,
        ssm_log_dt, ssm_b_re, ssm_b_im, ssm_c_re, ssm_c_im, ssm_d, w_glu, attn_out_g, ssm_out_g,
        w_out, ln2_g, w_ff_gate, w_ff_up, w_ff_down,
    )
    return second_block(
        x, norm_mix_pre_2, norm_mix_post_2, norm_mlp_pre_2, norm_mlp_post_2, w_in_ab_2,
        w_spatial_2, b_spatial_2, conv_w_2, w_out_ab_2, w_qkv_2, w_o_2, w_up_2, w_down_2,
    )


_drawn_inputs = setup_inputs


def setup_inputs(seed=0):
    import zlib

    import numpy as np

    out = dict(_drawn_inputs(seed))
    spreads = {}
    factors = {'ssm_a_re': 200.0,
     'ssm_a_im': 30.728,
     'ssm_log_dt': 32.424,
     'ssm_b_re': 42.064,
     'ssm_b_im': 42.336,
     'ssm_c_re': 42.448,
     'ssm_c_im': 42.296}
    for name, (base, spread) in spreads.items():
        noise = np.random.default_rng([zlib.crc32(name.encode()), seed]).standard_normal(out[name].shape)
        drawn = base * np.exp(spread * noise) if base else spread * noise
        out[name] = jnp.asarray(drawn.astype(out[name].dtype))
    for name, factor in factors.items():
        out[name] = (out[name] * factor).astype(out[name].dtype)
    return out
```

```python
from contextlib import ExitStack

import numpy as np

import concourse.bass as bass
from concourse import mybir

F32 = mybir.dt.float32
F32R = mybir.dt.float32r
ALU = mybir.AluOpType
ACT = mybir.ActivationFunctionType
X = mybir.AxisListType.X

D = 2048
HID1 = 5632
HID2 = 8192
EPS = 1e-6
LN_EPS = 1e-5
MAGIC = float(1.5 * 2 ** 23)
TWO_PI = 2.0 * np.pi
NEG = -1.0e30
NRAW = 3
NSPLIT = 3
LA = NSPLIT - 1
STATE_TILES = 32
SBUF_FROM = 16512
SBUF_TO = 229344

COLS = {}
_n = 0
for _name, _w in (("ln1", 16), ("ln2", 16), ("pre0", 16), ("pre1", 16), ("mpre0", 16), ("mpre1", 16),
                  ("attn_g", 8), ("ssm_g", 8), ("qg", 1), ("kg", 1), ("d", 8), ("a_re", 32), ("a_im", 32),
                  ("ldt", 32), ("conv", 24), ("bs", 8), ("sinks", 16)):
    COLS[_name] = (_n, _n + _w)
    _n += _w
NPAR = _n


def bcast(ap, axis, n):
    dims = [list(d) for d in ap.ap]
    dims.insert(axis, [0, n])
    return bass.AP(ap.tensor, ap.offset, dims)


class Engine:

    def __init__(self, sem, eng, serial=False):
        self.sem, self.eng, self.serial, self.n, self.seen = sem, eng, serial, 0, {}

    def wait(self, *tokens):
        for t in tokens:
            if t is None:
                continue
            if isinstance(t, list):
                self.wait(*t)
                continue
            sem, value = t
            if self.seen.get(id(sem), 0) < value:
                self.seen[id(sem)] = value
                if self.eng is not None:
                    self.eng.wait_ge(sem, value)

    def do(self, fn, *tokens, sig=True):
        self.wait(*tokens)
        if self.serial:
            self.wait(self.last())
        ins = fn(self.eng) if self.eng is not None else None
        if not sig:
            return None
        self.n += 1
        if ins is not None:
            ins.then_inc(self.sem, 1)
        return (self.sem, self.n)

    def last(self):
        return (self.sem, self.n) if self.n else None


class Region:

    def __init__(self, at):
        self.base = self.at = at

    def clear(self):
        self.at = self.base


class Banks:

    def __init__(self, banks):
        self.banks, self.at, self.free, self.held = list(banks), 0, {b: [] for b in banks}, set()

    def take(self):
        for _ in self.banks:
            b = self.banks[self.at % len(self.banks)]
            self.at += 1
            if b not in self.held:
                self.held.add(b)
                return b, self.free[b]
        raise RuntimeError("no bank is free")

    def done(self, b, tokens):
        self.held.discard(b)
        self.free[b] = tokens


def program(nc, inp, out, scratch):
    made = {}
    with ExitStack() as ctx:
        ps = ctx.enter_context(nc.psum_tensor("PS", [128, 8, 512], F32))
        schedule(nc, ctx, made, ps, inp, out, scratch, None, None)
        with nc.Block() as block:
            @block.sync
            def _(e):
                schedule(nc, ctx, made, ps, inp, out, scratch, "sync", e)

            @block.scalar
            def _(e):
                schedule(nc, ctx, made, ps, inp, out, scratch, "scalar", e)

            @block.vector
            def _(e):
                schedule(nc, ctx, made, ps, inp, out, scratch, "vector", e)

            @block.gpsimd
            def _(e):
                schedule(nc, ctx, made, ps, inp, out, scratch, "gpsimd", e)

            @block.tensor
            def _(e):
                schedule(nc, ctx, made, ps, inp, out, scratch, "tensor", e)


def schedule(nc, ctx, made, PS, inp, out, scratch, walk, eng):
    names = [0]

    keep = Region(SBUF_FROM)

    def sb(shape, dt=F32, stack=None, name="t"):
        names[0] += 1
        r = stack or keep
        n = 4
        for d in shape[1:]:
            n *= d
        key = f"{name}{names[0]}"
        if key not in made:
            made[key] = nc.alloc_sbuf_tensor_at(key, list(shape), dt, offset=r.at)
        h = made[key]
        r.at += -(-n // 64) * 64
        assert r.at <= SBUF_TO, (name, r.at)
        return h

    def sem(name):
        if name not in made:
            made[name] = ctx.enter_context(nc.semaphore(name))
        return made[name]

    XR = sb([128, 2, D], name="XR")
    kpa_at = keep.at
    KPA = sb([128, 16, 2, 256], F32R, name="KPA")
    RAW = sb([128, NRAW, 2, 1024], name="RAW")
    HI = sb([128, NSPLIT, 1024], F32R, name="HI")
    LO = sb([128, NSPLIT, 1024], F32R, name="LO")
    ACC = sb([128, 2, D], name="ACC")
    PAR = sb([128, NPAR], name="PAR")
    ID = sb([128, 128], name="ID")
    ST = sb([128, 384], name="ST")

    pe = Engine(sem("pe_done"), eng if walk == "tensor" else None)
    act = Engine(sem("act_done"), eng if walk == "scalar" else None)
    dve = Engine(sem("dve_done"), eng if walk == "vector" else None)
    pool = Engine(sem("pool_done"), eng if walk == "gpsimd" else None, serial=True)
    sp = Engine(None, eng if walk == "sync" else None)
    s_raw = [sem(f"raw_loaded{i}") for i in range(NRAW)]
    raw_n = [0] * NRAW
    loads = [0]

    def load(dst, src, *tokens):
        s = sem(f"load{loads[0]}")
        loads[0] += 1
        sp.wait(*tokens)
        sp.do(lambda e: e.dma_start(dst, src).then_inc(s, 16), sig=False)
        return (s, 16)

    def par(name, i=0, n=None):
        a, b = COLS[name]
        return PAR[:, a + i:(a + i + n) if n else b]

    st_at = [0]

    def small(n):
        a = st_at[0]
        st_at[0] += n
        assert st_at[0] <= 384
        return ST[:, a:a + n]

    def all_done():
        return [t for t in (pe.last(), act.last(), dve.last(), pool.last()) if t]

    steps = []
    dmas = []

    def unit(srcs, k0, nk, korder=None):
        width = sum(w for _, _, w in srcs)
        u = dict(width=width, nk=nk, first=len(steps), order=list(korder or range(nk)))
        i = 0
        while i < nk:
            n = 2 if i + 1 < nk and u["order"][i + 1] == u["order"][i] + 1 else 1
            parts = []
            at = 0
            for dram, c0, w in srcs:
                r = (k0 + u["order"][i]) * 128
                parts.append((at, w, dram[r:r + 128 * n, c0:c0 + w].rearrange("(k p) c -> p k c", p=128)))
                at += w
            dmas.append(dict(parts=parts, n=n, first=len(steps)))
            for j in range(n):
                steps.append(dict(dma=len(dmas) - 1, j=j, width=width))
            i += n
        return u

    state = dict(dma=0, split=0)
    pe_step = {}
    split_tok = {}

    def issue_dma():
        d = state["dma"]
        if d >= len(dmas):
            return
        m = dmas[d]
        slot = d % NRAW
        if d >= NRAW:
            prev = dmas[d - NRAW]
            for j in range(prev["n"]):
                sp.wait(*split_tok[prev["first"] + j])
        for at, w, src in m["parts"]:
            raw_n[slot] += 16
            dst = RAW[:, slot, 0:m["n"], at:at + w]
            sp.do(lambda e, dst=dst, src=src: e.dma_start(dst, src).then_inc(s_raw[slot], 16), sig=False)
        m["tok"] = (s_raw[slot], raw_n[slot])
        state["dma"] += 1

    def split_to(i):
        while state["split"] <= min(i, len(steps) - 1):
            s = state["split"]
            st = steps[s]
            m = dmas[st["dma"]]
            slot, h, w = st["dma"] % NRAW, s % NSPLIT, st["width"]
            src = RAW[:, slot, st["j"], 0:w]
            free = pe_step.get(s - NSPLIT)
            a = act.do(lambda e: e.activation(HI[:, h, 0:w], src, ACT.Copy), m["tok"], free)
            v = dve.do(lambda e: e.tensor_tensor(LO[:, h, 0:w], src, HI[:, h, 0:w].bitcast(F32), ALU.subtract),
                       a, m["tok"], free)
            split_tok[s] = (a, v)
            state["split"] += 1
            if st["j"] == m["n"] - 1:
                issue_dma()

    KT = {}

    def kslot(i):
        return (KPA, i) if i < 16 else (KT["b"], i - 16)

    free_pairs = []
    pair_free = {}

    def take_pair():
        p = free_pairs.pop(0)
        return p, pair_free.get(p, [])

    def give(slots, tok):
        for p in sorted({s // 2 for s, _ in slots}):
            pair_free[p] = [tok]
            free_pairs.append(p)

    main = Banks([0, 2, 4])
    side = Banks([6, 7])

    def run(u, chunks, evac, sides=(), every=1):
        w, nb = u["width"], (u["width"] + 511) // 512
        b0, f0 = main.take()
        b1, f1 = main.take()
        toks = [None, None]
        for i in range(u["nk"]):
            s = u["first"] + i
            split_to(s + LA)
            h = s % NSPLIT
            slot, ready = chunks[u["order"][i]]
            kt, ks = kslot(slot)
            for t, (b, f) in enumerate(((b0, f0), (b1, f1))):
                pe.wait(*split_tok[s], ready)
                if i == 0:
                    pe.wait(f)
                hi = kt[:, ks, 0, t * 128:(t + 1) * 128]
                lo = kt[:, ks, 1, t * 128:(t + 1) * 128]
                for j in range(nb):
                    cw = min(512, w - 512 * j)
                    o, c = PS[:, b + j, 0:cw], slice(512 * j, 512 * j + cw)
                    pe.do(lambda e, o=o, c=c, hi=hi, st=(i == 0): e.matmul(o, hi, HI[:, h, c], start=st, stop=False),
                          sig=False)
                    pe.do(lambda e, o=o, c=c, hi=hi: e.matmul(o, hi, LO[:, h, c], start=False, stop=False), sig=False)
                for j in range(nb):
                    cw = min(512, w - 512 * j)
                    o, c = PS[:, b + j, 0:cw], slice(512 * j, 512 * j + cw)
                    end = i == u["nk"] - 1
                    fn = lambda e, o=o, c=c, lo=lo, end=end: e.matmul(o, lo, HI[:, h, c], start=False, stop=end)
                    if j == nb - 1 and (t == 1 or end):
                        toks[t] = pe.do(fn)
                        if t == 1:
                            pe_step[s] = toks[1]
                    else:
                        pe.do(fn, sig=False)
            if i % every == every - 1:
                for g in sides:
                    next(g, None)
        for t, b in enumerate((b0, b1)):
            main.done(b, evac(t, b, toks[t]))
        return toks[1]

    def finish(g):
        for _ in g:
            pass

    def feed(srcs, gain, got, ready):
        n = len(ready)
        for c in range(0, n, 2):
            bank, fr = side.take()
            pe.wait(fr)
            for q in range(2):
                for t in range(2):
                    o = PS[:, bank, q * 256 + t * 128:q * 256 + t * 128 + 128]
                    s = srcs(c + q, t)
                    tk = pe.do(lambda e, o=o, s=s: e.transpose(o, s, ID[:, :]), ready[c + q], t_id,
                               sig=(q == 1 and t == 1))
            pair, pf = take_pair()
            kt, ks = kslot(2 * pair)
            if gain is None:
                src = PS[:, bank, :].rearrange("p (a b) -> p a b", a=2)
                a = act.do(lambda e: e.activation(kt[:, ks:ks + 2, 0, :], src, ACT.Copy), tk, pf)
                v = dve.do(lambda e: e.tensor_tensor(kt[:, ks:ks + 2, 1, :], src,
                                                     kt[:, ks:ks + 2, 0, :].bitcast(F32), ALU.subtract), a, tk, pf)
            else:
                for q in range(2):
                    src = PS[:, bank, q * 256:q * 256 + 256]
                    g = par(gain, c + q, 1)
                    a = act.do(lambda e: e.activation(kt[:, ks + q, 0, :], src, ACT.Copy, scale=g), tk, pf, t_par)
                for q in range(2):
                    src = PS[:, bank, q * 256:q * 256 + 256]
                    g = par(gain, c + q, 1)
                    v = dve.do(lambda e: e.scalar_tensor_tensor(
                        out=kt[:, ks + q, 1, :], in0=src, scalar=g, in1=kt[:, ks + q, 0, :].bitcast(F32),
                        op0=ALU.mult, op1=ALU.subtract), a, tk, pf, t_par)
            side.done(bank, [a, v])
            for q in range(2):
                got.append((2 * pair + q, [a, v]))
            yield

    def feed_split(srcs, got, n, ready):
        for c in range(0, n, 2):
            pair, pf = take_pair()
            kt, ks = kslot(2 * pair)
            src = srcs(c)
            a = act.do(lambda e: e.activation(kt[:, ks:ks + 2, 0, :], src, ACT.Copy), ready[c], ready[c + 1], pf)
            v = dve.do(lambda e: e.tensor_tensor(kt[:, ks:ks + 2, 1, :], src,
                                                 kt[:, ks:ks + 2, 0, :].bitcast(F32), ALU.subtract),
                       a, ready[c], ready[c + 1], pf)
            for q in range(2):
                got.append((2 * pair + q, [a, v]))
            yield

    def inv_root(dst, ssq, n, count, eps, *tokens):
        tmp = small(n)
        a = pool.do(lambda e: e.tensor_scalar(tmp, ssq, 1.0 / count, eps, ALU.mult, ALU.add), *tokens)
        return pool.do(lambda e: e.tensor_tensor(dst, tmp, NEG5[:, 0:n], ALU.pow), a, t_n5)

    def add_small(dst, a, b, *tokens):
        return pool.do(lambda e: e.tensor_tensor(dst, a, b, ALU.add), *tokens)

    t_x = [load(XR[:, t, :], inp["x"][t * 128:(t + 1) * 128, :]) for t in range(2)]
    t_id = load(ID[:, :], inp["ident"])
    t_par = load(PAR[:, :], inp["params"])

    w_in, w_out = inp["w_in"], inp["w_out"]
    U = {}
    U["u"] = unit([(w_in, 1536, 1024)], 0, 16)
    U["q"] = unit([(w_in, 0, 1024)], 0, 16)
    U["kv"] = unit([(w_in, 1024, 512)], 0, 16)
    U["wa"] = [unit([(w_out, 1024 * i, 1024)], 0, 8) for i in range(2)]
    U["glu"] = unit([(inp["w_glu"], 0, 1024)], 0, 8)
    U["ws"] = [unit([(w_out, 1024 * i, 1024)], 8, 8) for i in range(2)]
    nu = HID1 // 512
    U["up1"], U["dn1"] = [None] * nu, {}

    def up1(i):
        U["up1"][i] = unit([(inp["w_ff_gate"], 512 * i, 512), (inp["w_ff_up"], 512 * i, 512)], 0, 16)

    order1 = []
    for blk in range((nu + 1) // 2):
        for i in range(2 * blk, min(2 * blk + 2, nu)):
            up1(i)
            order1.append(("up", i))
        if blk:
            U["dn1"][blk - 1] = [unit([(inp["w_ff_down"], 1024 * c, 1024)], 8 * (blk - 1), 8) for c in range(2)]
            order1.append(("dn", blk - 1))
    blk = (nu + 1) // 2 - 1
    U["dn1"][blk] = [unit([(inp["w_ff_down"], 1024 * c, 1024)], 8 * blk, 2 * (HID1 // 256) - 8 * blk) for c in range(2)]
    order1.append(("dn", blk))
    wab = inp["w_in_ab"]
    U["ab"] = [unit([(wab, 1024 * c, 1024)], 0, 16) for c in (1, 3, 4, 2, 0)]
    U["oab"] = [unit([(inp["w_out_ab"], 1024 * c, 1024)], 0, 16, list(range(8, 16)) + list(range(8))) for c in range(2)]

    def ffn2_units(layer):
        ups, dns, order = [], [], []
        for b in range(HID2 // 1024):
            ups.append(unit([(inp["w_up"][layer], 1024 * b, 1024)], 0, 16))
            order.append(("up", b))
            if b:
                dns.append([unit([(inp["w_down"][layer], 1024 * c, 1024)], 8 * (b - 1), 8) for c in range(2)])
                order.append(("dn", b - 1))
        b = HID2 // 1024 - 1
        dns.append([unit([(inp["w_down"][layer], 1024 * c, 1024)], 8 * b, 8) for c in range(2)])
        order.append(("dn", b))
        return ups, dns, order

    F2 = [ffn2_units(0)]
    U["qkv"] = [[unit([(inp["w_qkv"], 2048 * p + 1024 * hf, 1024)], 0, 16) for p in range(3)] for hf in range(2)]
    U["wo"] = [[unit([(inp["w_o"], 1024 * c, 1024)], 8 * hf, 8) for c in range(2)] for hf in range(2)]
    F2.append(ffn2_units(1))

    for _ in range(NRAW):
        issue_dma()

    free_pairs.extend(range(8))

    NEG5 = sb([128, 48], name="NEG5")
    t_n5 = pool.do(lambda e: e.memset(NEG5[:, :], -0.5))
    kb_region = Region(keep.at)
    ph = Region(keep.at + 32768)
    u_sb = ACC[:, 0, :].rearrange("p (t c) -> p t c", t=2)
    uT = ACC[:, 1, :].rearrange("p (k c) -> p k c", k=8)
    yT = u_sb.rearrange("p t c -> p (t c)").rearrange("p (k c) -> p k c", k=8)
    WK = [sb([128, 512], stack=kb_region, name="WK") for _ in range(16)]
    q_sb = sb([128, 2, 1024], stack=ph, name="q_sb")
    kv_sb = sb([128, 2, 512], stack=ph, name="kv_sb")
    upper = Region(kpa_at + 16384)
    qT = sb([128, 8, 256], stack=upper, name="qT")
    kT = sb([128, 4, 256], stack=upper, name="kT")
    KD = sb([128, 2, 4, 128], stack=upper, name="KD")
    BL = sb([128, 2, 8, 128], stack=ph, name="BL")
    CL = sb([128, 2, STATE_TILES, 32], stack=ph, name="CL")
    JK = sb([128, 1024], stack=ph, name="JK")
    BT = sb([128, 4, 384], stack=ph, name="BT")
    TAU = sb([128, 256], stack=ph, name="TAU")
    SP_ = sb([128, 16, 32], stack=ph, name="SPR")

    t_tau = load(TAU[:, :], inp["tau"])
    t_cl = load(CL[:, :, :, :].rearrange("p a b c -> p (a b c)"), inp["ssm_c"])
    t_cl = dve.do(lambda e: e.tensor_scalar(CL[:, 1, :, :], CL[:, 1, :, :], -1.0, None, ALU.mult), t_cl)

    ss = small(2)
    r1 = small(2)
    junk = None
    for t in range(2):
        for hf in range(2):
            pass
    xs4 = small(4)
    for t in range(2):
        for hf in range(2):
            junk = act.do(lambda e, t=t, hf=hf: e.activation(JK[:, :], XR[:, t, hf * 1024:hf * 1024 + 1024], ACT.Square,
                                                            accum_out=xs4[:, hf * 2 + t:hf * 2 + t + 1]),
                          t_x[t], junk)
    a = add_small(ss, xs4[:, 0:2], xs4[:, 2:4], junk)
    t_r1 = inv_root(r1, ss, 2, D, EPS, a)
    xT = []
    fd = feed(lambda c, t: XR[:, t, c * 128:(c + 1) * 128], "ln1", xT, [t_x] * 16)
    finish(fd)

    def to_sb(dst, r, tr):
        toks = [None, None]

        def evac(t, b, tok):
            d = dst(t)
            w = d.shape[-1]
            src = PS[:, b:b + (w // 512), :].rearrange("p a b -> p (a b)")
            toks[t] = act.do(lambda e: e.activation(d, src, ACT.Copy, scale=r[:, t:t + 1]), tok, tr)
            return [toks[t]]
        evac.toks = toks
        return evac

    sp_i = [0]

    def spt():
        sp_i[0] += 1
        return SP_[:, sp_i[0] - 1, :]

    BN, BX = WK[0], WK[2]
    bn_re, bn_im = WK[0], WK[1]
    t_bn = [load(bn_re[:, :], inp["ssm_b"][0]), load(bn_im[:, :], inp["ssm_b"][1])]
    E_ = sb([128, 1], stack=ph, name="EB")
    HP = sb([128, 1], stack=ph, name="HP")
    EB = E_[:, 0:1]
    t_e = pool.do(lambda e: e.memset(EB, float(np.e)))
    t_hp = pool.do(lambda e: e.memset(HP[:, :], float(np.pi / 2)))
    mag, qf, fre, fim, dt_, ang, v1, v2, v3, v4, v5, v6 = [spt() for _ in range(12)]
    are, aim = par("a_re"), par("a_im")
    eb = bcast(EB, 1, 32)
    eb = bass.AP(E_[:, 0:1].tensor, E_[:, 0:1].offset, [list(E_[:, 0:1].ap[0]), [0, 32]])
    a = pool.do(lambda e: e.tensor_tensor(dt_, eb, par("ldt"), ALU.pow), t_e, t_par)
    a = pool.do(lambda e: e.tensor_tensor(v1, are, dt_, ALU.mult), a)
    p_ang = pool.do(lambda e: e.tensor_tensor(ang, aim, dt_, ALU.mult), a)
    p_mag = pool.do(lambda e: e.tensor_tensor(mag, eb, v1, ALU.pow), p_ang)
    inv2pi = 1.0 / TWO_PI
    c1 = float(np.float32(6.28125))
    c2 = float(np.float32(TWO_PI - 6.28125)) if False else float(0.0019350051879882812)
    c3 = TWO_PI - c1 - c2
    v = dve.do(lambda e: e.tensor_scalar(v2, ang, inv2pi, None, ALU.mult), p_ang)
    v = dve.do(lambda e: e.tensor_scalar(v3, v2, MAGIC, -MAGIC, ALU.add, ALU.add), v)
    v = dve.do(lambda e: e.scalar_tensor_tensor(out=v4, in0=v3, scalar=-c1, in1=ang, op0=ALU.mult, op1=ALU.add), v)
    v = dve.do(lambda e: e.scalar_tensor_tensor(out=v5, in0=v3, scalar=-c2, in1=v4, op0=ALU.mult, op1=ALU.add), v)
    v = dve.do(lambda e: e.scalar_tensor_tensor(out=v4, in0=v3, scalar=-c3, in1=v5, op0=ALU.mult, op1=ALU.add), v)
    v = dve.do(lambda e: e.tensor_scalar(v5, v4, 3.1415925, -3.1415925, ALU.min, ALU.max), v)
    t_qf = dve.do(lambda e: e.tensor_scalar(qf, v4, inv2pi, None, ALU.mult), v)
    a = act.do(lambda e: e.activation(v6, v5, ACT.Sin), v)
    a = act.do(lambda e: e.activation(v3, v5, ACT.Sin, scale=0.5), t_qf)
    v = dve.do(lambda e: e.scalar_tensor_tensor(out=v1, in0=v3, scalar=-2.0, in1=v3, op0=ALU.mult, op1=ALU.mult), a, p_mag)
    v = dve.do(lambda e: e.tensor_scalar(v2, v1, 1.0, None, ALU.add), v)
    v = dve.do(lambda e: e.scalar_tensor_tensor(out=v3, in0=mag, scalar=-1.0, in1=v2, op0=ALU.add, op1=ALU.mult), v)
    v = dve.do(lambda e: e.tensor_tensor(v2, v3, v1, ALU.add), v)
    v = dve.do(lambda e: e.tensor_tensor(v4, mag, v6, ALU.mult), v)
    v = dve.do(lambda e: e.tensor_tensor(v1, are, are, ALU.mult), v)
    v = dve.do(lambda e: e.tensor_tensor(v3, aim, aim, ALU.mult), v)
    v = dve.do(lambda e: e.tensor_tensor(v5, v1, v3, ALU.add), v)
    v = dve.do(lambda e: e.reciprocal(v1, v5), v)
    v = dve.do(lambda e: e.tensor_tensor(v3, v2, are, ALU.mult), v)
    v = dve.do(lambda e: e.tensor_tensor(v5, v4, aim, ALU.mult), v)
    v = dve.do(lambda e: e.tensor_tensor(v6, v3, v5, ALU.add), v)
    v = dve.do(lambda e: e.tensor_tensor(fre, v6, v1, ALU.mult), v)
    v = dve.do(lambda e: e.tensor_tensor(v3, v4, are, ALU.mult), v)
    v = dve.do(lambda e: e.tensor_tensor(v5, v2, aim, ALU.mult), v)
    v = dve.do(lambda e: e.tensor_tensor(v6, v3, v5, ALU.subtract), v)
    t_f = dve.do(lambda e: e.tensor_tensor(fim, v6, v1, ALU.mult), v)

    def b3(t):
        return t[:, :].rearrange("p (j c) -> p j c", c=16)

    frb, fib = bcast(fre, 2, 16), bcast(fim, 2, 16)
    T1, T2 = WK[2], WK[3]
    XB = [(WK[4], WK[5]), (WK[6], WK[7])]
    z = [dve.do(lambda e, w=w: e.memset(w[:, :], 0.0)) for pr in XB for w in pr]
    TS = WK[8]
    t_xb = []
    for part, (fa, fb, op) in enumerate(((frb, fib, ALU.subtract), (fib, frb, ALU.add))):
        v = dve.do(lambda e: e.tensor_tensor(b3(T1), b3(bn_re), fa, ALU.mult), t_bn, t_f)
        v = dve.do(lambda e: e.tensor_tensor(b3(T2), b3(bn_im), fb, ALU.mult), v)
        v = dve.do(lambda e: e.tensor_tensor(TS[:, :], T1[:, :], T2[:, :], op), v)
        for hf in range(2):
            dst = XB[part][hf]
            for g in range(2):
                o = dst[64 * g:64 * g + 64, :].rearrange("p (j c) -> p j c", c=32)[:, :, 16 * g:16 * g + 16]
                s = TS[64 * g:64 * g + 64, :].rearrange("p (j c) -> p j c", c=16)[:, 16 * hf:16 * hf + 16, :]
                w = dve.do(lambda e: e.tensor_copy(o, s), v, z)
        v = w
        t_xb.append(w)
        t_f = w
    t_bl = [None, None]
    for part in range(2):
        for hf in range(2):
            bank, fr = side.take()
            for q in range(4):
                o = PS[:, bank, q * 128:(q + 1) * 128]
                s = XB[part][hf][:, q * 128:(q + 1) * 128]
                tk = pe.do(lambda e, o=o, s=s: e.transpose(o, s, ID[:, :]), fr, t_xb[part], t_id, sig=(q == 3))
            d = BL[:, part, 4 * hf:4 * hf + 4, :].rearrange("p a b -> p (a b)")
            a = act.do(lambda e: e.activation(d, PS[:, bank, :], ACT.Copy), tk)
            side.done(bank, [a])
            t_bl[part] = a

    RB, OH = WK[9][0:33, 0:16], WK[10][0:33, 0:383]
    t_rb = load(RB[0:32, :], inp["rel_bias"])
    t_rb2 = pool.do(lambda e: e.memset(RB[32:33, :], 1.0))
    t_oh = load(OH, inp["onehot"])
    WV = JK
    bank, fr = side.take()
    t_wv = tk = pe.do(lambda e: e.matmul(PS[0:16, bank, 0:383], RB, OH, start=True, stop=True), fr, t_rb, t_rb2, t_oh)
    a = act.do(lambda e: e.activation(WV[0:16, 0:383], PS[0:16, bank, 0:383], ACT.Copy), tk, junk)
    side.done(bank, [a])
    junk = a
    s_w = sem("bias_written")
    sp.wait(a)
    sp.do(lambda e: e.dma_start(scratch[:, :, 0:383], bcast(WV[0:16, 0:383], 1, 128)).then_inc(s_w, 16), sig=False)
    t_w = (s_w, 16)

    ev = to_sb(lambda t: u_sb[:, t, :], r1, t_r1)
    run(U["u"], xT, ev)
    t_u = ev.toks
    t_uT = []

    def u_turn():
        for c in range(0, 8, 2):
            bank, fr = side.take()
            for q in range(2):
                for t in range(2):
                    o = PS[:, bank, q * 256 + t * 128:q * 256 + t * 128 + 128]
                    s = u_sb[:, t, (c + q) * 128:(c + q + 1) * 128]
                    tk = pe.do(lambda e, o=o, s=s: e.transpose(o, s, ID[:, :]), fr, t_u[t], sig=(q == 1 and t == 1))
            d = uT[:, c:c + 2, :].rearrange("p a b -> p (a b)")
            a = act.do(lambda e: e.activation(d, PS[:, bank, :], ACT.Copy), tk)
            side.done(bank, [a])
            t_uT.extend([a, a])
            yield

    t_y = []

    def ssm_side():
        yield from u_turn()
        last = {}
        for b in range(16):
            kc, hh = b // 2, b % 2
            w = WK[8 * (b % 2):8 * (b % 2) + 8]
            old = last.get(b % 2)
            j0 = 2 * b
            phi, rnd, sn, cs, g_re, g_im, m1, m2 = w

            def t3(x):
                return x[:, :].rearrange("p (j c) -> p j c", j=2)
            p = pool.do(lambda e: e.tensor_tensor(t3(phi), bcast(qf[:, j0:j0 + 2], 2, 256),
                                                  bcast(TAU[:, :], 1, 2), ALU.mult), t_qf, t_tau, t_xb, t_bl, t_wv, old)
            v = dve.do(lambda e: e.tensor_scalar(rnd[:, :], phi[:, :], MAGIC, -MAGIC, ALU.add, ALU.add), p)
            p = pool.do(lambda e: e.tensor_tensor(sn[:, :], phi[:, :], rnd[:, :], ALU.subtract), v)
            a = act.do(lambda e: e.activation(phi[:, :], sn[:, :], ACT.Abs), p)
            a1 = act.do(lambda e: e.activation(rnd[:, :], sn[:, :], ACT.Sin, scale=6.283185), p)
            a2 = act.do(lambda e: e.activation(cs[:, :], phi[:, :], ACT.Sin, scale=-6.283185, bias=HP[:, 0:1]), a, t_hp)
            sn2 = rnd
            br, fr = side.take()
            bi, fi = side.take()
            tk = None
            for i in range(2):
                pe.wait(tk)
                for part, bk, ff in ((0, br, fr), (1, bi, fi)):
                    r0 = 64 * hh + 32 * i
                    l = BL[r0:r0 + 32, part, kc, :]
                    rr = uT[r0:r0 + 32, kc, :]
                    o = PS[:, bk, i * 256:(i + 1) * 256]
                    tk = pe.do(lambda e: e.matmul(o, l, rr, start=True, stop=True), ff, t_bl[part], t_uT[kc])
            yield
            ure, uim = PS[:, br, :], PS[:, bi, :]
            free = sn
            v1_ = dve.do(lambda e: e.tensor_tensor(m1[:, :], cs[:, :], ure, ALU.mult), a2, a1, tk)
            v2_ = dve.do(lambda e: e.tensor_tensor(m2[:, :], sn2[:, :], uim, ALU.mult))
            p1 = pool.do(lambda e: e.tensor_tensor(m1[:, :], m1[:, :], m2[:, :], ALU.add), v2_)
            v3_ = dve.do(lambda e: e.tensor_tensor(phi[:, :], cs[:, :], uim, ALU.mult))
            v4_ = dve.do(lambda e: e.tensor_tensor(sn[:, :], sn2[:, :], ure, ALU.mult))
            side.done(br, [v4_])
            side.done(bi, [v4_])
            p2 = pool.do(lambda e: e.tensor_tensor(m2[:, :], phi[:, :], sn[:, :], ALU.subtract), v4_, p1)
            yield
            for src, dst, pp in ((m1, g_re, p1), (m2, g_im, p2)):
                for i in range(2):
                    dcy = bass.AP(mag.tensor, mag[:, j0 + i:j0 + i + 1].offset, [list(mag.ap[0]), [0, 256]])
                    c = slice(256 * i, 256 * i + 256)
                    v = dve.do(lambda e: e.tensor_tensor_scan(dst[:, c], dcy, src[:, c], 0.0, ALU.mult, ALU.add), pp)
            yield
            P1, P2, P3, P4 = m1, phi, sn, m2
            va = dve.do(lambda e: e.tensor_tensor(P1[:, :], cs[:, :], g_re[:, :], ALU.mult), v)
            pd = pool.do(lambda e: e.tensor_tensor(P4[:, :], cs[:, :], g_im[:, :], ALU.mult), v)
            vb = dve.do(lambda e: e.scalar_tensor_tensor(out=P2[:, :], in0=g_im[:, :], scalar=-1.0, in1=sn2[:, :],
                                                         op0=ALU.mult, op1=ALU.mult), p2)
            vc = dve.do(lambda e: e.tensor_tensor(P3[:, :], sn2[:, :], g_re[:, :], ALU.mult))
            yield
            by, fy = side.take()
            for i in range(2):
                r0 = 64 * hh + 32 * i
                o = PS[r0:r0 + 32, by, 0:256]
                c = slice(256 * i, 256 * i + 256)
                for n, (P, part) in enumerate(((P1, 0), (P2, 0), (P3, 1), (P4, 1))):
                    l = CL[:, part, j0 + i, :]
                    tk = pe.do(lambda e, o=o, l=l, P=P, c=c, n=n: e.matmul(o, l, P[:, c], start=(n == 0), stop=(n == 3),
                                                                        tile_position=(0, r0)),
                               fy, va, vb, vc, pd, t_cl, sig=(i == 1 and n == 3))
            last[b % 2] = [tk]
            yield
            h0 = slice(64 * hh, 64 * hh + 64)
            yb = slice(256 * (kc % 4), 256 * (kc % 4) + 256)
            v = dve.do(lambda e: e.scalar_tensor_tensor(out=JK[h0, yb], in0=uT[h0, kc, :], scalar=par("d", kc, 1)[h0, :],
                                                        in1=PS[h0, by, 0:256], op0=ALU.mult, op1=ALU.add),
                       tk, t_par, t_w, t_uT[7], t_y[-4] if len(t_y) >= 4 else None)
            side.done(by, [v])
            if hh == 1:
                y = act.do(lambda e: e.activation(yT[:, kc, :], JK[:, 256 * (kc % 4):256 * (kc % 4) + 256],
                                                  ACT.Gelu_apprx_tanh), v)
                t_y.append(y)
            yield

    main.banks, main.at = [0, 2], 0
    side.free[4] = main.free[4]
    side.free[5] = main.free[4]
    side.banks = [4, 5, 6, 7]
    for b in (0, 1, 2, 3):
        side.free.setdefault(b, [])
    S1 = ssm_side()
    evq = to_sb(lambda t: q_sb[:, t, :], r1, t_r1)
    run(U["q"], xT, evq, [S1], 1)
    evk = to_sb(lambda t: kv_sb[:, t, :], r1, t_r1)
    tl = run(U["kv"], xT, evk, [S1], 1)
    give(xT, tl)

    sqs = small(32)
    rq = small(32)
    sks = small(8)
    rk = small(8)
    t_q, t_k = evq.toks, evk.toks
    qn, kn = [None, None], [None, None]
    SQ = sb([128, 1024], stack=ph, name="SQ")

    def heads(ap, n):
        return ap.rearrange("p (h d) -> p h d", h=n)

    pv_ = None
    for t in range(2):
        a = act.do(lambda e: e.activation(SQ[:, :], q_sb[:, t, :], ACT.Square), t_q[t], pv_)
        v = dve.do(lambda e: e.tensor_reduce(sqs[:, 16 * t:16 * t + 16], heads(SQ[:, :], 16), X, ALU.add), a)
        a = act.do(lambda e: e.activation(SQ[:, 0:256], kv_sb[:, t, 0:256], ACT.Square), t_k[t], v)
        pv_ = dve.do(lambda e: e.tensor_reduce(sks[:, 4 * t:4 * t + 4], heads(SQ[:, 0:256], 4), X, ALU.add), a)
    p1 = inv_root(rq, sqs, 32, 64, EPS, pv_)
    p2 = inv_root(rk, sks, 8, 64, EPS, pv_)
    for t in range(2):
        qn[t] = dve.do(lambda e: e.tensor_tensor(heads(q_sb[:, t, :], 16), heads(q_sb[:, t, :], 16),
                                                 bcast(rq[:, 16 * t:16 * t + 16], 2, 64), ALU.mult), p1, t_q[t])
        for dd in range(2):
            kn[t] = dve.do(lambda e: e.tensor_tensor(KD[:, t, :, 64 * dd:64 * dd + 64], heads(kv_sb[:, t, 0:256], 4),
                                                     bcast(rk[:, 4 * t:4 * t + 4], 2, 64), ALU.mult), p2, t_k[t])
    t_qT, t_kT = {}, {}

    def turn(src, dst, c, gain, *tokens):
        bank, fr = side.take()
        for q in range(2):
            for t in range(2):
                o = PS[:, bank, q * 256 + t * 128:q * 256 + t * 128 + 128]
                s = src(c + q, t)
                tk = pe.do(lambda e, o=o, s=s: e.transpose(o, s, ID[:, :]), fr, *tokens, sig=(q == 1 and t == 1))
        d = dst[:, c:c + 2, :].rearrange("p a b -> p (a b)")
        if gain is None:
            a = act.do(lambda e: e.activation(d, PS[:, bank, :], ACT.Copy), tk, *tokens)
        else:
            a = act.do(lambda e: e.activation(d, PS[:, bank, :], ACT.Copy, scale=gain), tk, *tokens)
        side.done(bank, [a])
        return a

    def attn_prep():
        for c in (0, 2):
            t_kT[c] = t_kT[c + 1] = turn(lambda cc, t: KD[:, t, cc, :], kT, c, par("kg"), kn, t_par)
            yield
        for c in range(0, 8, 2):
            t_qT[c] = t_qT[c + 1] = turn(lambda cc, t: q_sb[:, t, cc * 128:(cc + 1) * 128], qT, c, par("qg"), qn, t_par)
            yield

    def attn_group(n, q_of, k_of, v_of, dv, scale, mask, tmask, sinks, write, LG, PT, stats, tr):
        mx, mm, ng, sm, sk, den, rc = stats
        tS = []
        for h in range(4):
            bank, fr = side.take()
            q, k, tq = q_of(h), k_of(h), tr[h]
            pe.do(lambda e: e.matmul(PS[:, bank, 0:128], q[:, 0:128], k[:, 0:128], start=True, stop=True), fr, tq, sig=False)
            tk = pe.do(lambda e: e.matmul(PS[:, bank, 128:384], q[:, 128:256], k, start=True, stop=True))
            mk = mask(h)
            v = dve.do(lambda e: e.scalar_tensor_tensor(out=LG[:, h, :], in0=PS[:, bank, 0:384], scalar=scale, in1=mk,
                                                        op0=ALU.mult, op1=ALU.add), tk, tmask, last_pt[h])
            side.done(bank, [v])
            tS.append(v)
            if h % 2:
                yield
        mx3 = mx.rearrange("p (h s) -> p h s", s=3)
        mm2 = mm.rearrange("p (h s) -> p h s", s=2)
        v = dve.do(lambda e: e.tensor_reduce(mx3, LG[:, :, :].rearrange("p h (s c) -> p h s c", s=3), X, ALU.max),
                   tS, last_st)
        v = dve.do(lambda e: e.tensor_tensor(mm2[:, :, 1], mx3[:, :, 1], mx3[:, :, 2], ALU.max), v)
        if sinks is not None:
            v = dve.do(lambda e: e.tensor_tensor(mm2[:, :, 1], mm2[:, :, 1], sinks, ALU.max), v)
            v = dve.do(lambda e: e.tensor_tensor(mm2[:, :, 0], mx3[:, :, 0], sinks, ALU.max), v)
        else:
            v = dve.do(lambda e: e.tensor_copy(mm2[:, :, 0], mx3[:, :, 0]), v)
        vn = dve.do(lambda e: e.tensor_scalar(ng, mm, -1.0, None, ALU.mult), v)
        if sinks is not None:
            v = dve.do(lambda e: e.tensor_tensor(sk.rearrange("p (h s) -> p h s", s=2), bcast(sinks, 2, 2),
                                                 ng.rearrange("p (h s) -> p h s", s=2), ALU.add), vn)
            ask = act.do(lambda e: e.activation(sk, sk, ACT.Exp), v)
        yield
        ta = []
        for h in range(4):
            for s, (c0, c1_) in enumerate(((0, 128), (128, 384))):
                a = act.do(lambda e: e.activation(LG[:, h, c0:c1_], LG[:, h, c0:c1_], ACT.Exp,
                                                  bias=ng[:, 2 * h + s:2 * h + s + 1],
                                                  accum_out=sm[:, 2 * h + s:2 * h + s + 1]), vn)
            ta.append(a)
            if h == 1:
                yield
        if sinks is not None:
            v = dve.do(lambda e: e.tensor_tensor(den, sm, sk, ALU.add), ta, ask)
        else:
            v = dve.do(lambda e: e.tensor_copy(den, sm), ta)
        tr_ = dve.do(lambda e: e.reciprocal(rc, den), v)
        yield
        per = 512 // (2 * dv)
        ob = None
        for h in range(4):
            bank, fr = side.take()
            for s in range(3):
                o, sr = PS[:, bank, s * 128:(s + 1) * 128], LG[:, h, s * 128:(s + 1) * 128]
                tk = pe.do(lambda e, o=o, sr=sr: e.transpose(o, sr, ID[:, :]), fr, ta[h], sig=(s == 2))
            last_pt[h] = tk
            if h % 2:
                c = dve.do(lambda e: e.tensor_copy(PT[:, h, :], PS[:, bank, 0:384]), tk, last_o[h])
            else:
                c = act.do(lambda e: e.activation(PT[:, h, :], PS[:, bank, 0:384], ACT.Copy), tk, last_o[h])
            side.done(bank, [c])
            yield
            if h % per == 0:
                ob, fo = side.take()
                pe.wait(fo)
            x0 = (h % per) * 2 * dv
            v0, v1x = v_of(h, 0), v_of(h, 1)
            pe.do(lambda e: e.matmul(PS[:, ob, x0:x0 + dv], PT[:, h, 0:128], v0, start=True, stop=True), c, sig=False)
            pe.do(lambda e: e.matmul(PS[:, ob, x0 + dv:x0 + 2 * dv], PT[:, h, 128:256], v0, start=True, stop=False), sig=False)
            tk = pe.do(lambda e: e.matmul(PS[:, ob, x0 + dv:x0 + 2 * dv], PT[:, h, 256:384], v1x, start=False, stop=True))
            last_o[h] = tk
            if h % per == per - 1:
                w = []
                for t in range(2):
                    src = PS[:, ob, :].rearrange("p (h t d) -> p t h d", t=2, d=dv)[:, t]
                    r = rc.rearrange("p (h s) -> p s h", s=2)[:, t, h - per + 1:h + 1]
                    w.append(write(t, h - per + 1, per, src, bcast(r, 2, dv), tk, tr_))
                side.done(ob, [w[-1]])
            yield
        last_st[:] = [w[-1]]

    last_pt, last_o, last_st = [None] * 4, [None] * 4, []
    LG = sb([128, 4, 384], stack=ph, name="LG")
    PT = sb([128, 4, 384], stack=ph, name="PT")

    def make_stats():
        n = small(12), small(8), small(8), small(8), small(8), small(8), small(8)
        return n

    stats = make_stats()
    t_bt = [None]
    t_att = {}

    def load_bias(g, *tokens):
        s = sem(f"bias{g}")
        sp.wait(t_w, *tokens)
        for h in range(4):
            for c0, n, off in ((0, 128, 128), (128, 256, 0)):
                src = bass.AP(scratch.tensor, (4 * g + h) * 128 * 384 + 127 + off, [[383, 128], [1, n]])
                dst = BT[:, h, c0:c0 + n]
                sp.do(lambda e, src=src, dst=dst: e.dma_start(dst, src).then_inc(s, 16), sig=False)
        return (s, 128)

    def attn1():
        yield from attn_prep()
        for g in range(4):
            tb = load_bias(g, list(last_st))

            def write(t, h0, per, src, r, tk, trr):
                c0 = (4 * g + h0) * 64
                d = heads(q_sb[:, t, c0:c0 + per * 64], per)
                t_att[(t, g)] = dve.do(lambda e: e.tensor_tensor(d, src, r, ALU.mult), tk, trr, list(t_qT.values()))
                return t_att[(t, g)]

            def q_of(h):
                b = 64 * (h % 2)
                return qT[b:b + 64, 2 * g + h // 2, :]

            def k_of(h):
                b = 64 * (h % 2)
                return kT[b:b + 64, g, :]
            yield from attn_group(g, q_of, k_of, lambda h, t: kv_sb[:, t, 256 + 64 * g:320 + 64 * g], 64, 0.125,
                                  lambda h: BT[:, h, :], tb, par("sinks", 4 * g, 4), write, LG, PT, stats,
                                  [[t_qT[2 * g + h // 2], t_kT[g], t_k] for h in range(4)])

    A1 = attn1()
    alive = [A1, S1]

    def drain(*gens):
        gens = list(gens)
        while gens:
            for g in list(gens):
                try:
                    next(g)
                except StopIteration:
                    gens.remove(g)

    def drive(first, *others):
        for _ in first:
            for g in others:
                next(g, None)

    drive(A1, S1)
    asq, rA = small(2), small(2)
    for t in range(2):
        a = act.do(lambda e: e.activation(SQ[:, :], q_sb[:, t, :], ACT.Square, accum_out=asq[:, t:t + 1]),
                   [t_att[(t, g)] for g in range(4)], a)
    t_rA = inv_root(rA, asq, 2, 1024, EPS, a)
    oT = []
    finish(feed(lambda c, t: q_sb[:, t, c * 128:(c + 1) * 128], "attn_g", oT,
                [[t_att[(0, c // 2)], t_att[(1, c // 2)]] for c in range(8)]))
    xr_tok = {}

    def add_x(c, r, tr):
        def evac(t, b, tok):
            d = XR[:, t, c * 1024:(c + 1) * 1024]
            src = PS[:, b:b + 2, :].rearrange("p a b -> p (a b)")
            if r is None:
                v = dve.do(lambda e: e.tensor_tensor(d, src, d, ALU.add), tok, xr_tok.get((t, c)))
            else:
                v = dve.do(lambda e: e.scalar_tensor_tensor(out=d, in0=src, scalar=r[:, t:t + 1], in1=d,
                                                            op0=ALU.mult, op1=ALU.add), tok, tr, xr_tok.get((t, c)))
            xr_tok[(t, c)] = v
            return [v]
        return evac

    for c in range(2):
        tl = run(U["wa"][c], oT, add_x(c, rA, t_rA), [S1])
    give(oT, tl)
    finish(S1)

    gate = all_done()
    kb_region.clear()
    KT["b"] = sb([128, 16, 2, 256], F32R, stack=kb_region, name="KPB")
    for p in range(4, 8):
        pair_free[p] = gate
    for p in range(8, 16):
        pair_free[p] = gate
        free_pairs.append(p)

    yk = []
    finish(feed_split(lambda c: yT[:, c:c + 2, :], yk, 8, t_y))
    ys = q_sb
    t_ys = [None, None]
    t_sg = {}

    def ev_glu(t, b, tok):
        src = PS[:, b:b + 2, :].rearrange("p a b -> p (a b)")
        t_sg[t] = act.do(lambda e: e.activation(ys[:, t, :], src, ACT.Sigmoid), tok, [x[1] for x in oT], pe.last())
        return [t_sg[t]]

    tl = run(U["glu"], yk, ev_glu)
    give(yk, tl)
    for t in range(2):
        for hf in range(2):
            bank, fr = side.take()
            for q in range(4):
                c = 4 * hf + q
                o, s = PS[:, bank, q * 128:(q + 1) * 128], yT[:, c, t * 128:(t + 1) * 128]
                tk = pe.do(lambda e, o=o, s=s: e.transpose(o, s, ID[:, :]), fr, t_y, sig=(q == 3))
            d = ys[:, t, 512 * hf:512 * hf + 512]
            t_ys[t] = dve.do(lambda e: e.tensor_tensor(d, d, PS[:, bank, :], ALU.mult), tk, t_sg[t])
            side.done(bank, [t_ys[t]])
    gsq, rS = small(2), small(2)
    for t in range(2):
        a = act.do(lambda e: e.activation(SQ[:, :], ys[:, t, :], ACT.Square, accum_out=gsq[:, t:t + 1]), t_ys[t], a)
    t_rS = inv_root(rS, gsq, 2, 1024, EPS, a)
    sT = []
    finish(feed(lambda c, t: ys[:, t, c * 128:(c + 1) * 128], "ssm_g", sT, [t_ys] * 8))

    side.banks = [6, 7]
    main.banks = [0, 2, 4]
    main.at = 0
    main.free[4] = side.free[4] + side.free[5]

    def sq_part(src, t, dst, jk, *tokens):
        return act.do(lambda e: e.activation(jk, src, ACT.Square, accum_out=dst), *tokens)

    def new_norm(gain):
        return dict(gain=gain, part=small(4), r=small(2), got=[], jt=None)

    jk_tok = [junk]

    def norm_cols(nm, c):
        def g():
            rd = [[xr_tok[(0, c)], xr_tok[(1, c)]]] * 8
            for t in range(2):
                jk_tok[0] = act.do(lambda e: e.activation(JK_[0][:, :], XR[:, t, c * 1024:(c + 1) * 1024], ACT.Square,
                                                          accum_out=nm["part"][:, 2 * c + t:2 * c + t + 1]),
                                   xr_tok[(t, c)], jk_tok[0])
            nm["jt"] = jk_tok[0]
            if c == 1:
                a = add_small(nm["ss"], nm["part"][:, 0:2], nm["part"][:, 2:4], nm["jt"])
                nm["tr"] = inv_root(nm["r"], nm["ss"], 2, D, EPS, a)
            g0 = nm["gain"]
            COLS["_"] = (COLS[g0][0] + 8 * c, COLS[g0][0] + 8 * c + 8)
            COLS[(g0, c)] = COLS["_"]
            yield from feed(lambda i, t: XR[:, t, (8 * c + i) * 128:(8 * c + i + 1) * 128], (g0, c), nm["got"], rd)
        return g()

    JK_ = [JK]
    nm2 = new_norm("ln2")
    nm2["ss"] = small(2)
    run(U["ws"][0], sT, add_x(0, rS, t_rS))
    n0 = norm_cols(nm2, 0)
    tl = run(U["ws"][1], sT, add_x(1, rS, t_rS), [n0])
    finish(n0)
    finish(norm_cols(nm2, 1))
    give(sT, tl)

    def phase():
        g = all_done()
        for e in (pe, act, dve, pool, sp):
            e.wait(*g)
        ph.clear()

    phase()
    JK_[0] = sb([128, 1024], stack=ph, name="JK")
    HS = [sb([128, 2, 1024], stack=ph, name="HS") for _ in range(2)]
    SG = [sb([128, 512], stack=ph, name="SG") for _ in range(2)]
    hs_read = [None, None]
    sg_read = [None, None]
    hid = {}

    def up1_run(i, sides):
        H, half = HS[(i // 2) % 2], i % 2
        tk_h = [None, None]

        def evac(t, b, tok):
            d = H[:, t, 512 * half:512 * half + 512]
            a = act.do(lambda e: e.activation(SG[t][:, :], PS[:, b, :], ACT.Silu, scale=nm2["r"][:, t:t + 1]),
                       tok, nm2["tr"], sg_read[t])
            tk_h[t] = sg_read[t] = dve.do(lambda e: e.scalar_tensor_tensor(
                out=d, in0=PS[:, b + 1, :], scalar=nm2["r"][:, t:t + 1], in1=SG[t][:, :], op0=ALU.mult, op1=ALU.mult),
                tok, a, nm2["tr"], hs_read[(i // 2) % 2])
            return [a, tk_h[t]]
        run(U["up1"][i], nm2["got"], evac, sides)
        return H, half, tk_h

    pend = []
    for kind, i in order1:
        if kind == "up":
            H, half, tk_h = up1_run(i, pend)
            for g in pend:
                finish(g)
            got = hid.setdefault(i // 2, [])

            def g_(H=H, half=half, tk_h=tk_h, got=got, i=i):
                yield from feed(lambda c, t: H[:, t, 512 * half + c * 128:512 * half + (c + 1) * 128], None, got, [tk_h] * 4)
                hs_read[(i // 2) % 2] = pe.last()
            pend = [g_()]
            if i == nu - 1:
                give(nm2["got"], pe.last())
        else:
            lastb = i == (nu + 1) // 2 - 1
            if lastb:
                for g in pend:
                    finish(g)
                pend = []
                nm3 = new_norm("pre0")
                nm3["ss"] = small(2)
            for c in range(2):
                tl = run(U["dn1"][i][c], hid[i], add_x(c, None, None), pend)
                for g in pend:
                    finish(g)
                pend = []
                if lastb and c == 0:
                    pend = [norm_cols(nm3, 0)]
            give(hid[i], tl)
    finish(norm_cols(nm3, 1))

    phase()
    JK_[0] = sb([128, 1024], stack=ph, name="JK")
    AV = sb([128, 2, 1024], stack=ph, name="AV")
    GC = sb([128, 2, 1024], stack=ph, name="GC")
    GB = sb([128, 2, 1024], stack=ph, name="GB")
    ZT = sb([128, 8, 258], stack=ph, name="ZT")
    WS = sb([128, 8, 128], stack=ph, name="WS")
    CM = sb([128, 128], stack=ph, name="CM")
    CV = [sb([128, 256], stack=ph, name="CV") for _ in range(3)]
    BO = sb([128, 2, 256], stack=ph, name="BO")
    t_ws = load(WS[:, :, :], inp["w_spatial"].rearrange("s (g t) -> s g t", g=8))
    t_cm = load(CM[:, :], inp["causal"])
    t_wm = dve.do(lambda e: e.tensor_tensor(WS[:, :, :], WS[:, :, :], bcast(CM[:, :], 1, 8), ALU.mult), t_ws, t_cm)
    t_zz = dve.do(lambda e: e.memset(ZT[:, :, 0:2], 0.0))
    mu2, vs2, rv2 = small(2), small(2), small(2)
    t_vn = [None, None]
    rr, trr = nm3["r"], nm3["tr"]

    def flat2(b):
        return PS[:, b:b + 2, :].rearrange("p a b -> p (a b)")

    def ev_av(t, b, tok):
        a0 = act.do(lambda e: e.activation(AV[:, t, :], flat2(b), ACT.Gelu_apprx_tanh, scale=rr[:, t:t + 1],
                                           accum_out=mu2[:, t:t + 1]), tok, trr)
        v = dve.do(lambda e: e.tensor_scalar(mu2[:, t:t + 1], mu2[:, t:t + 1], -1.0 / 1024, None, ALU.mult), a0)
        v = dve.do(lambda e: e.tensor_scalar(AV[:, t, :], AV[:, t, :], mu2[:, t:t + 1], None, ALU.add), v)
        jk_tok[0] = act.do(lambda e: e.activation(JK_[0][:, :], AV[:, t, :], ACT.Square, accum_out=vs2[:, t:t + 1]),
                           v, jk_tok[0])
        if t == 1:
            p = inv_root(rv2, vs2, 2, 1024, LN_EPS, jk_tok[0])
            for tt in range(2):
                t_vn[tt] = dve.do(lambda e: e.tensor_scalar(AV[:, tt, :], AV[:, tt, :], rv2[:, tt:tt + 1], None, ALU.mult), p)
        return [a0]

    run(U["ab"][0], nm3["got"], ev_av)
    t_mx = {}

    def mixing():
        for t in range(2):
            for hf in range(2):
                bank, fr = side.take()
                for q in range(4):
                    g = 4 * hf + q
                    o = PS[:, bank, q * 128:(q + 1) * 128]
                    tk = pe.do(lambda e, o=o, g=g: e.matmul(o, WS[:, g, :], AV[:, t, g * 128:(g + 1) * 128],
                                                            start=True, stop=True), fr, t_wm, t_vn[t], sig=(q == 3))
                d = AV[:, t, 512 * hf:512 * hf + 512].rearrange("p (g c) -> p g c", g=4)
                s = PS[:, bank, :].rearrange("p (g c) -> p g c", g=4)
                t_mx[t] = dve.do(lambda e: e.tensor_tensor(d, s, bcast(par("bs", 4 * hf, 4), 2, 128), ALU.add), tk)
                side.done(bank, [t_mx[t]])
                yield

    evg = to_sb(lambda t: GC[:, t, :], rr, trr)
    mxg = mixing()
    run(U["ab"][1], nm3["got"], evg, [mxg])
    t_z = [None, None]

    def ev_z(t, b, tok):
        t_z[t] = dve.do(lambda e: e.scalar_tensor_tensor(out=GC[:, t, :], in0=flat2(b), scalar=rr[:, t:t + 1],
                                                         in1=GC[:, t, :], op0=ALU.mult, op1=ALU.mult),
                        tok, evg.toks[t])
        return [t_z[t]]
    run(U["ab"][2], nm3["got"], ev_z)
    finish(mxg)
    t_zT = {}

    def z_turn():
        for c in range(0, 8, 2):
            bank, fr = side.take()
            for q in range(2):
                for t in range(2):
                    o = PS[:, bank, q * 256 + t * 128:q * 256 + t * 128 + 128]
                    s = GC[:, t, (c + q) * 128:(c + q + 1) * 128]
                    tk = pe.do(lambda e, o=o, s=s: e.transpose(o, s, ID[:, :]), fr, t_z[t], sig=(q == 1 and t == 1))
            a = act.do(lambda e: e.activation(ZT[:, c:c + 2, 2:258], PS[:, bank, :].rearrange("p (a b) -> p a b", a=2),
                                              ACT.Copy), tk)
            side.done(bank, [a])
            t_zT[c] = t_zT[c + 1] = a
            yield
    zg = z_turn()
    evb = to_sb(lambda t: GB[:, t, :], rr, trr)
    run(U["ab"][3], nm3["got"], evb, [zg])
    finish(zg)
    bk_ = []
    ak_ = []

    def conv_side():
        prev = None
        for c in range(0, 8, 2):
            bank, fr = side.take()
            for q in range(2):
                for t in range(2):
                    o = PS[:, bank, q * 256 + t * 128:q * 256 + t * 128 + 128]
                    s = GB[:, t, (c + q) * 128:(c + q + 1) * 128]
                    tk = pe.do(lambda e, o=o, s=s: e.transpose(o, s, ID[:, :]), fr, evb.toks[t], sig=(q == 1 and t == 1))
            for q in range(2):
                k = c + q
                cw = [par("conv", 8 * tap + k, 1) for tap in range(3)]
                v = dve.do(lambda e: e.tensor_scalar(CV[0][:, :], ZT[:, k, 0:256], cw[0], None, ALU.mult), t_zT[k], t_zz, prev)
                v = dve.do(lambda e: e.scalar_tensor_tensor(out=CV[1][:, :], in0=ZT[:, k, 1:257], scalar=cw[1],
                                                            in1=CV[0][:, :], op0=ALU.mult, op1=ALU.add), v)
                v = dve.do(lambda e: e.scalar_tensor_tensor(out=CV[2][:, :], in0=ZT[:, k, 2:258], scalar=cw[2],
                                                            in1=CV[1][:, :], op0=ALU.mult, op1=ALU.add), v)
                v = dve.do(lambda e: e.tensor_tensor(BO[:, q, :], CV[2][:, :], PS[:, bank, q * 256:q * 256 + 256],
                                                     ALU.mult), v, tk)
                prev = v
            side.done(bank, [v])
            pair, pf = take_pair()
            kt, ks = kslot(2 * pair)
            a = act.do(lambda e: e.activation(kt[:, ks:ks + 2, 0, :], BO[:, :, :], ACT.Copy), v, pf)
            prev = dve.do(lambda e: e.tensor_tensor(kt[:, ks:ks + 2, 1, :], BO[:, :, :],
                                                    kt[:, ks:ks + 2, 0, :].bitcast(F32), ALU.subtract), a, pf)
            for q in range(2):
                bk_.append((2 * pair + q, [a, prev]))
            yield
    cg = conv_side()
    t_ao = [None, None]

    def ev_au(t, b, tok):
        a = act.do(lambda e: e.activation(GC[:, t, :], flat2(b), ACT.Gelu_apprx_tanh, scale=rr[:, t:t + 1]),
                   tok, t_zT[7])
        t_ao[t] = dve.do(lambda e: e.tensor_tensor(GC[:, t, :], GC[:, t, :], AV[:, t, :], ALU.mult), a, t_mx[t])
        return [a]
    tl = run(U["ab"][4], nm3["got"], ev_au, [cg])
    finish(cg)
    give(nm3["got"], tl)
    finish(feed(lambda c, t: GC[:, t, c * 128:(c + 1) * 128], None, ak_, [t_ao] * 8))

    GP = sb([128, D], stack=ph, name="GP")
    acc_tok = {}

    def post(name, idx, dst_g):
        return load(dst_g[:, :], inp[name][idx:idx + 1, :].partition_broadcast(128).rearrange("p a c -> p (a c)"))

    def post_state():
        return dict(part=small(4), ss=small(2), r=small(2))

    def ev_post(c, psn, g, tg, add):
        def evac(t, b, tok):
            d = ACC[:, t, c * 1024:(c + 1) * 1024]
            if add:
                v0 = dve.do(lambda e: e.tensor_tensor(d, flat2(b), d, ALU.add), tok, acc_tok.get((t, c)))
            else:
                v0 = dve.do(lambda e: e.tensor_copy(d, flat2(b)), tok, acc_tok.get((t, c)))
            jk_tok[0] = act.do(lambda e: e.activation(JK_[0][:, :], d, ACT.Square,
                                                      accum_out=psn["part"][:, 2 * c + t:2 * c + t + 1]), v0, jk_tok[0])
            acc_tok[(t, c)] = dve.do(lambda e: e.tensor_tensor(d, d, g[:, c * 1024:(c + 1) * 1024], ALU.mult),
                                     v0, tg, jk_tok[0])
            psn["jt"] = jk_tok[0]
            return [v0]
        return evac

    def post_add(psn):
        a = add_small(psn["ss"], psn["part"][:, 0:2], psn["part"][:, 2:4], psn["jt"])
        p = inv_root(psn["r"], psn["ss"], 2, D, EPS, a)
        for c in range(2):
            for t in range(2):
                s, d = ACC[:, t, c * 1024:(c + 1) * 1024], XR[:, t, c * 1024:(c + 1) * 1024]
                xr_tok[(t, c)] = dve.do(lambda e: e.scalar_tensor_tensor(out=d, in0=s, scalar=psn["r"][:, t:t + 1], in1=d,
                                                                         op0=ALU.mult, op1=ALU.add),
                                        p, acc_tok[(t, c)], xr_tok.get((t, c)))
                acc_tok[(t, c)] = xr_tok[(t, c)]

    tg = post("norm_mix_post", 0, GP)
    psn = post_state()
    ch = ak_ + bk_
    for c in range(2):
        tl = run(U["oab"][c], ch, ev_post(c, psn, GP, tg, False))
    give(ch, tl)
    post_add(psn)

    def norm_both(gain):
        nm = new_norm(gain)
        nm["ss"] = small(2)
        finish(norm_cols(nm, 0))
        finish(norm_cols(nm, 1))
        return nm

    def ffn2(nm, layer):
        ups, dns, order = F2[layer]
        H = [sb([128, 2, 1024], stack=ph, name="HS") for _ in range(2)]
        RL = sb([128, 1024], stack=ph, name="RL")
        G = sb([128, D], stack=ph, name="GP")
        tgg = post("norm_mlp_post", layer, G)
        psn = post_state()
        rd = [None, None]
        rl_tok = [None]
        hid2 = {}
        pend = []
        for kind, b in order:
            if kind == "up":
                Hb = H[b % 2]
                th = [None, None]

                def evac(t, bk, tok):
                    a = act.do(lambda e: e.activation(RL[:, :], flat2(bk), ACT.Relu, scale=nm["r"][:, t:t + 1]),
                               tok, nm["tr"], rl_tok[0])
                    rl_tok[0] = th[t] = dve.do(lambda e: e.tensor_tensor(Hb[:, t, :], RL[:, :], RL[:, :], ALU.mult),
                                               a, rd[b % 2])
                    return [a]
                run(ups[b], nm["got"], evac, pend)
                for g in pend:
                    finish(g)
                if b == len(ups) - 1:
                    give(nm["got"], pe.last())
                got = hid2.setdefault(b, [])

                def g_(Hb=Hb, th=th, got=got, b=b):
                    yield from feed(lambda c, t: Hb[:, t, c * 128:(c + 1) * 128], None, got, [th] * 8)
                    rd[b % 2] = pe.last()
                pend = [g_()]
                if b == 0:
                    pass
            else:
                final = b == len(ups) - 1
                if final:
                    for g in pend:
                        finish(g)
                    pend = []
                for c in range(2):
                    if final:
                        ev = ev_post(c, psn, G, tgg, True)
                    else:
                        def ev(t, bk, tok, c=c):
                            d = ACC[:, t, c * 1024:(c + 1) * 1024]
                            if b == 0:
                                v = dve.do(lambda e: e.tensor_copy(d, flat2(bk)), tok, acc_tok.get((t, c)))
                            else:
                                v = dve.do(lambda e: e.tensor_tensor(d, flat2(bk), d, ALU.add), tok, acc_tok.get((t, c)))
                            acc_tok[(t, c)] = v
                            return [v]
                    tl = run(dns[b][c], hid2[b], ev, pend)
                for g in pend:
                    finish(g)
                pend = []
                give(hid2[b], tl)
        post_add(psn)

    nm4 = norm_both("mpre0")
    phase()
    JK_[0] = sb([128, 1024], stack=ph, name="JK")
    ffn2(nm4, 0)

    nm5 = norm_both("pre1")
    phase()
    JK_[0] = sb([128, 1024], stack=ph, name="JK")
    q2 = sb([128, 8, 256], stack=ph, name="q2T")
    k2 = sb([128, 8, 256], stack=ph, name="k2T")
    v2_ = [ACC[:, h, :].rearrange("p (t c) -> p t c", t=2) for h in range(2)]
    TK = sb([128, 2, 1024], stack=ph, name="TK")
    M1 = sb([128, 512], stack=ph, name="M1")
    M2 = sb([128, 512], stack=ph, name="M2")
    CS = sb([128, 2, 2, 64], stack=ph, name="CS")
    DM = sb([128, 384], stack=ph, name="DM")
    LG = sb([128, 4, 384], stack=ph, name="LG")
    PT = sb([128, 4, 384], stack=ph, name="PT")
    OS = sb([128, 2, 1024], stack=ph, name="OS")
    t_cs = load(CS[:, :, :, :].rearrange("p a b c -> p (a b c)"), inp["rope"])
    t_dm = load(DM[:, :], inp["dilmask"])
    t_rc = None
    for t in range(2):
        c_ = CS[:, t, :, :].rearrange("p a b -> p (a b)")
        t_rc = dve.do(lambda e: e.tensor_scalar(c_, c_, nm5["r"][:, t:t + 1], None, ALU.mult), t_cs, nm5["tr"])
    stats2 = stats
    last_pt[:] = [None] * 4
    last_o[:] = [None] * 4
    last_st[:] = []
    tk_free = [None]
    m_free = [None]

    def ev_rope(toks):
        def evac(t, b, tok):
            ps4 = flat2(b).rearrange("p (h s d) -> p h s d", h=8, s=2)
            o4 = TK[:, t, :].rearrange("p (h s d) -> p h s d", h=8, s=2)
            m1, m2 = M1[:, :].rearrange("p (h d) -> p h d", h=8), M2[:, :].rearrange("p (h d) -> p h d", h=8)
            cs, sn = bcast(CS[:, t, 0, :], 1, 8), bcast(CS[:, t, 1, :], 1, 8)
            a_, b_ = ps4[:, :, 0, :], ps4[:, :, 1, :]
            dve.do(lambda e: e.tensor_tensor(o4[:, :, 0, :], a_, cs, ALU.mult), tok, t_rc, tk_free[0])
            va = dve.do(lambda e: e.tensor_tensor(m1, b_, sn, ALU.mult), m_free[0])
            p = pool.do(lambda e: e.tensor_tensor(o4[:, :, 0, :], o4[:, :, 0, :], m1, ALU.subtract), va)
            dve.do(lambda e: e.tensor_tensor(o4[:, :, 1, :], b_, cs, ALU.mult))
            vb = dve.do(lambda e: e.tensor_tensor(m2, a_, sn, ALU.mult))
            p = pool.do(lambda e: e.tensor_tensor(o4[:, :, 1, :], o4[:, :, 1, :], m2, ALU.add), vb)
            toks[t] = p
            m_free[0] = p
            return [vb]
        return evac

    tT = [{}, {}]

    def turn8(dst, which, toks, busy):
        for c in range(0, 8, 2):
            a = turn(lambda cc, t: TK[:, t, cc * 128:(cc + 1) * 128], dst, c, None, list(toks), busy)
            tT[which][c] = tT[which][c + 1] = a
            tk_free[0] = pe.last()
            yield
    os_free = [None]
    oks = [[], []]
    t_os = {}

    def attn2(hf, tv):
        tr_now = [dict(tT[0]), dict(tT[1])]
        for g in range(2):
            def write(t, h0, per, src, r, tk, trr):
                c0 = (4 * g + h0) * 128
                d = OS[:, t, c0:c0 + per * 128].rearrange("p (h d) -> p h d", h=per)
                t_os[(hf, t, 4 * g + h0)] = dve.do(lambda e: e.tensor_tensor(d, src, r, ALU.mult), tk, trr, os_free[0])
                return t_os[(hf, t, 4 * g + h0)]
            yield from attn_group(g, lambda h: q2[:, 4 * g + h, :], lambda h: k2[:, 4 * g + h, :],
                                  lambda h, t: v2_[hf][:, t, (4 * g + h) * 128:(4 * g + h + 1) * 128], 128,
                                  128.0 ** -0.5, lambda h: DM[:, :], t_dm, None, write, LG, PT, stats2,
                                  [[tr_now[0][4 * g + h], tr_now[1][4 * g + h], tv] for h in range(4)])
            yield from feed(lambda c, t: OS[:, t, (4 * g + c) * 128:(4 * g + c + 1) * 128], None, oks[hf],
                            [[t_os[(hf, 0, 4 * g + 2 * (c // 2))], t_os[(hf, 1, 4 * g + 2 * (c // 2))]] for c in range(4)])
        os_free[0] = pe.last()

    main.banks, main.at = [0, 2], 0
    side.free[4] = list(main.free[4])
    side.free[5] = list(main.free[4])
    side.banks = [4, 5, 6, 7]
    prev_attn = None
    for hf in range(2):
        tq, tkk = [None, None], [None, None]
        sides = [prev_attn] if prev_attn else []
        run(U["qkv"][hf][0], nm5["got"], ev_rope(tq), sides)
        if prev_attn:
            finish(prev_attn)
        gq = turn8(q2, 0, tq, [pe.last()] if hf else None)
        finish(gq)
        run(U["qkv"][hf][1], nm5["got"], ev_rope(tkk))
        gk = turn8(k2, 1, tkk, [pe.last()] if hf else None)
        ev = to_sb(lambda t: v2_[hf][:, t, :], nm5["r"], nm5["tr"])
        act.wait(list(acc_tok.values()))
        tl = run(U["qkv"][hf][2], nm5["got"], ev, [gk])
        finish(gk)
        prev_attn = attn2(hf, ev.toks)
    give(nm5["got"], tl)
    CS2 = {}
    W2 = sb([128, 2, D], stack=ph, name="OW") if False else None
    JP = {}
    finish(prev_attn)
    gate = all_done()
    for t in range(2):
        for c in range(2):
            acc_tok[(t, c)] = gate
    main.banks, main.at = [0, 2, 4], 0
    main.free[4] = side.free[4] + side.free[5]
    side.banks = [6, 7]
    for c in range(2):
        def ev(t, bk, tok, c=c):
            d = ACC[:, t, c * 1024:(c + 1) * 1024]
            v = dve.do(lambda e: e.tensor_copy(d, flat2(bk)), tok, acc_tok[(t, c)])
            acc_tok[(t, c)] = v
            return [v]
        tl = run(U["wo"][0][c], oks[0], ev)
    give(oks[0], tl)
    phase()
    JK_[0] = sb([128, 1024], stack=ph, name="JK")
    GP2 = sb([128, D], stack=ph, name="GP")
    tg = post("norm_mix_post", 1, GP2)
    psn = post_state()
    for c in range(2):
        tl = run(U["wo"][1][c], oks[1], ev_post(c, psn, GP2, tg, True))
    give(oks[1], tl)
    post_add(psn)
    nm6 = norm_both("mpre1")
    ffn2(nm6, 1)

    s_out = sem("out_written")
    for c in range(2):
        for t in range(2):
            sp.wait(xr_tok[(t, c)])
            s, d = XR[:, t, c * 1024:(c + 1) * 1024], out[t * 128:(t + 1) * 128, c * 1024:(c + 1) * 1024]
            sp.do(lambda e, s=s, d=d: e.dma_start(d, s).then_inc(s_out, 16), sig=False)
    sp.wait((s_out, 64), (s_w, 16))
    assert state["split"] == len(steps) and state["dma"] == len(dmas)


def _buckets():
    dist = np.arange(128)
    nf = np.maximum(dist, 1).astype(np.float32)
    large = 16 + (np.log(nf / 16) / np.log(128 / 16) * 16).astype(np.int32)
    return np.where(dist < 16, dist, np.minimum(large, 31)).astype(np.int32)


def constants():
    c = {"ident": np.eye(128, dtype=np.float32)}
    onehot = np.zeros((33, 383), np.float32)
    bk = _buckets()
    for x in range(383):
        dist = 255 - x
        if 0 <= dist < 128:
            onehot[bk[dist], x] = 1.0
        else:
            onehot[32, x] = NEG
    c["onehot"] = onehot
    c["tau"] = np.ascontiguousarray(np.broadcast_to(np.arange(256, dtype=np.float32), (128, 256)))
    c["causal"] = np.triu(np.ones((128, 128), np.float32))
    half = 64
    inv = (np.float32(10000.0) ** (-np.arange(half, dtype=np.float32) * np.float32(2.0) / np.float32(128))).astype(np.float32)
    angle = np.arange(256, dtype=np.float32)[:, None] * inv[None, :]
    cs = np.stack([np.cos(angle.astype(np.float64)), np.sin(angle.astype(np.float64))], 1).astype(np.float32)
    c["rope"] = np.ascontiguousarray(cs.reshape(2, 128, 2, half).transpose(1, 0, 2, 3).reshape(128, 256))
    t = np.arange(256)[:, None]
    j = np.arange(256)[None, :]
    d = t - j
    count = ((d >= 0) & (d <= 128)).astype(int) + ((d >= 0) & (d % 4 == 0)) + ((d >= 0) & (d % 16 == 0))
    lc = np.where(count > 0, np.log(np.maximum(count, 1)), NEG).astype(np.float32)
    c["dilmask"] = np.ascontiguousarray(np.concatenate([lc[:128, :128], lc[128:, :]], 1))
    return c


def kernel(**inputs):
    import concourse.bacc as _bacc
    from concourse.bass_utils import run_bass_kernel_spmd as _run

    f = {k: np.asarray(v) for k, v in inputs.items()}
    feat = lambda a, n: a.reshape(n, 128).T
    states = lambda a: a.reshape(32, 128).T
    rep = lambda a: np.broadcast_to(a, (128, a.shape[-1]))
    p = np.zeros((128, NPAR), np.float32)

    def put(name, a):
        p[:, COLS[name][0]:COLS[name][1]] = a
    put("ln1", feat(f["ln1_g"][0], 16))
    put("ln2", feat(f["ln2_g"][0], 16))
    for l in range(2):
        put(f"pre{l}", feat(f["norm_mix_pre_2"][l], 16))
        put(f"mpre{l}", feat(f["norm_mlp_pre_2"][l], 16))
    put("attn_g", feat(f["attn_out_g"][0], 8))
    put("ssm_g", feat(f["ssm_out_g"][0], 8))
    put("qg", np.concatenate([f["q_norm_g"][0]] * 2)[:, None])
    put("kg", np.concatenate([f["k_norm_g"][0]] * 2)[:, None])
    put("d", feat(f["ssm_d"][0], 8))
    put("a_re", states(f["ssm_a_re"][0]))
    put("a_im", states(f["ssm_a_im"][0]))
    put("ldt", states(np.repeat(f["ssm_log_dt"][0], 64)))
    put("conv", f["conv_w_2"][0].reshape(3, 8, 128).transpose(2, 0, 1).reshape(128, 24))
    put("bs", f["b_spatial_2"][0].T)
    put("sinks", rep(f["attn_sinks"][0]))

    b = np.stack([f["ssm_b_re"][0], f["ssm_b_im"][0]]).reshape(2, 32, 128, 16).transpose(0, 2, 1, 3).reshape(2, 128, 512)
    cc = np.zeros((2, 64, 2, 32, 2, 16), np.float32)
    for i, name in enumerate(("ssm_c_re", "ssm_c_im")):
        a = f[name][0].reshape(32, 2, 16, 64)
        for g in range(2):
            cc[g, :, i, :, g, :] = a[:, g].transpose(2, 0, 1)
    arrays = {
        "x": f["x"][0], "w_in": f["w_in"][0], "w_glu": f["w_glu"][0], "w_out": f["w_out"][0],
        "w_ff_gate": f["w_ff_gate"][0], "w_ff_up": f["w_ff_up"][0], "w_ff_down": f["w_ff_down"][0],
        "w_in_ab": f["w_in_ab_2"][0], "w_out_ab": f["w_out_ab_2"][0], "w_qkv": f["w_qkv_2"][0], "w_o": f["w_o_2"][0],
        "w_up": f["w_up_2"], "w_down": f["w_down_2"], "rel_bias": f["rel_bias"],
        "norm_mix_post": f["norm_mix_post_2"], "norm_mlp_post": f["norm_mlp_post_2"],
        "params": p, "ssm_b": b, "ssm_c": cc.reshape(128, 2048),
        "w_spatial": f["w_spatial_2"][0].transpose(2, 0, 1).reshape(128, 1024),
    }
    arrays.update(constants())
    nc = _bacc.Bacc("TRN2", target_bir_lowering=False, num_devices=1)
    feeds, inp = {}, {}
    for name, a in arrays.items():
        a = np.ascontiguousarray(a)
        feeds[f"in_{name}"] = a
        inp[name] = nc.dram_tensor(f"in_{name}", a.shape, mybir.dt.from_np(a.dtype), kind="ExternalInput").ap()
    out = nc.dram_tensor("out_x", (256, D), F32, kind="ExternalOutput").ap()
    scratch = nc.dram_tensor("bias_rows", (16, 128, 384), F32, kind="Internal").ap()
    program(nc, inp, out, scratch)
    r = _run(nc, [feeds], core_ids=[0])
    return r.results[0]["out_x"].reshape(1, 256, D)
```

```python
from contextlib import ExitStack

import numpy as np

import concourse.bass as bass
from concourse import mybir

F32 = mybir.dt.float32
F32R = mybir.dt.float32r
ALU = mybir.AluOpType
ACT = mybir.ActivationFunctionType
X = mybir.AxisListType.X

D = 2048
HID1 = 5632
HID2 = 8192
EPS = 1e-6
LN_EPS = 1e-5
MAGIC = float(1.5 * 2 ** 23)
TWO_PI = 2.0 * np.pi
NEG = -1.0e30
NRAW = 3
NSPLIT = 3
LA = NSPLIT - 1
FEED_AHEAD = 5
STATE_TILES = 32
SBUF_FROM = 16512
SBUF_TO = 229344

COLS = {}
_n = 0
for _name, _w in (("ln1", 16), ("ln2", 16), ("pre0", 16), ("pre1", 16), ("mpre0", 16), ("mpre1", 16),
                  ("attn_g", 8), ("ssm_g", 8), ("qg", 1), ("kg", 1), ("d", 8), ("a_re", 32), ("a_im", 32),
                  ("ldt", 32), ("conv", 24), ("bs", 8), ("sinks", 16)):
    COLS[_name] = (_n, _n + _w)
    _n += _w
NPAR = _n


def bcast(ap, axis, n):
    dims = [list(d) for d in ap.ap]
    dims.insert(axis, [0, n])
    return bass.AP(ap.tensor, ap.offset, dims)


class Engine:

    def __init__(self, sem, eng, serial=False):
        self.sem, self.eng, self.serial, self.n, self.seen = sem, eng, serial, 0, {}

    def wait(self, *tokens):
        for t in tokens:
            if t is None:
                continue
            if isinstance(t, list):
                self.wait(*t)
                continue
            sem, value = t
            if self.seen.get(id(sem), 0) < value:
                self.seen[id(sem)] = value
                if self.eng is not None:
                    self.eng.wait_ge(sem, value)

    def do(self, fn, *tokens, sig=True):
        self.wait(*tokens)
        if self.serial:
            self.wait(self.last())
        ins = fn(self.eng) if self.eng is not None else None
        if not sig:
            return None
        self.n += 1
        if ins is not None:
            ins.then_inc(self.sem, 1)
        return (self.sem, self.n)

    def last(self):
        return (self.sem, self.n) if self.n else None


class Region:

    def __init__(self, at):
        self.base = self.at = at

    def clear(self):
        self.at = self.base


class Banks:

    def __init__(self, banks):
        self.banks, self.at, self.free, self.held = list(banks), 0, {b: [] for b in banks}, set()

    def take(self):
        for _ in self.banks:
            b = self.banks[self.at % len(self.banks)]
            self.at += 1
            if b not in self.held:
                self.held.add(b)
                return b, self.free[b]
        raise RuntimeError("no bank is free")

    def done(self, b, tokens):
        self.held.discard(b)
        self.free[b] = tokens


def program(nc, inp, out, scratch):
    made = {}
    with ExitStack() as ctx:
        ps = ctx.enter_context(nc.psum_tensor("PS", [128, 8, 512], F32))
        schedule(nc, ctx, made, ps, inp, out, scratch, None, None)
        with nc.Block() as block:
            @block.sync
            def _(e):
                schedule(nc, ctx, made, ps, inp, out, scratch, "sync", e)

            @block.scalar
            def _(e):
                schedule(nc, ctx, made, ps, inp, out, scratch, "scalar", e)

            @block.vector
            def _(e):
                schedule(nc, ctx, made, ps, inp, out, scratch, "vector", e)

            @block.gpsimd
            def _(e):
                schedule(nc, ctx, made, ps, inp, out, scratch, "gpsimd", e)

            @block.tensor
            def _(e):
                schedule(nc, ctx, made, ps, inp, out, scratch, "tensor", e)


def schedule(nc, ctx, made, PS, inp, out, scratch, walk, eng):
    names = [0]

    keep = Region(SBUF_FROM)

    def sb(shape, dt=F32, stack=None, name="t"):
        names[0] += 1
        r = stack or keep
        n = 4
        for d in shape[1:]:
            n *= d
        key = f"{name}{names[0]}"
        if key not in made:
            made[key] = nc.alloc_sbuf_tensor_at(key, list(shape), dt, offset=r.at)
        h = made[key]
        r.at += -(-n // 64) * 64
        assert r.at <= SBUF_TO, (name, r.at)
        return h

    def sem(name):
        if name not in made:
            made[name] = ctx.enter_context(nc.semaphore(name))
        return made[name]

    XR = sb([128, 2, D], name="XR")
    kpa_at = keep.at
    KPA = sb([128, 16, 2, 256], F32R, name="KPA")
    RAW = sb([128, NRAW, 2, 1024], name="RAW")
    HI = sb([128, NSPLIT, 1024], F32R, name="HI")
    LO = sb([128, NSPLIT, 1024], F32R, name="LO")
    ACC = sb([128, 2, D], name="ACC")
    PAR = sb([128, NPAR], name="PAR")
    ID = sb([128, 128], name="ID")
    ST = sb([128, 384], name="ST")

    pe = Engine(sem("pe_done"), eng if walk == "tensor" else None)
    act = Engine(sem("act_done"), eng if walk == "scalar" else None)
    dve = Engine(sem("dve_done"), eng if walk == "vector" else None)
    pool = Engine(sem("pool_done"), eng if walk == "gpsimd" else None, serial=True)
    sp = Engine(None, eng if walk == "sync" else None)
    s_raw = [sem(f"raw_loaded{i}") for i in range(NRAW)]
    raw_n = [0] * NRAW
    loads = [0]

    def load(dst, src, *tokens):
        s = sem(f"load{loads[0]}")
        loads[0] += 1
        sp.wait(*tokens)
        sp.do(lambda e: e.dma_start(dst, src).then_inc(s, 16), sig=False)
        return (s, 16)

    def par(name, i=0, n=None):
        a, b = COLS[name]
        return PAR[:, a + i:(a + i + n) if n else b]

    st_at = [0]

    def small(n):
        a = st_at[0]
        st_at[0] += n
        assert st_at[0] <= 384
        return ST[:, a:a + n]

    def all_done():
        return [t for t in (pe.last(), act.last(), dve.last(), pool.last()) if t]

    steps = []
    dmas = []

    def unit(srcs, k0, nk, korder=None):
        width = sum(w for _, _, w in srcs)
        u = dict(width=width, nk=nk, first=len(steps), order=list(korder or range(nk)))
        i = 0
        while i < nk:
            n = 2 if i + 1 < nk and u["order"][i + 1] == u["order"][i] + 1 else 1
            parts = []
            at = 0
            for dram, c0, w in srcs:
                r = (k0 + u["order"][i]) * 128
                parts.append((at, w, dram[r:r + 128 * n, c0:c0 + w].rearrange("(k p) c -> p k c", p=128)))
                at += w
            dmas.append(dict(parts=parts, n=n, first=len(steps)))
            for j in range(n):
                steps.append(dict(dma=len(dmas) - 1, j=j, width=width))
            i += n
        return u

    state = dict(dma=0, split=0)
    pe_step = {}
    split_tok = {}

    def issue_dma():
        d = state["dma"]
        if d >= len(dmas):
            return
        m = dmas[d]
        slot = d % NRAW
        if d >= NRAW:
            prev = dmas[d - NRAW]
            for j in range(prev["n"]):
                sp.wait(*split_tok[prev["first"] + j])
        for at, w, src in m["parts"]:
            raw_n[slot] += 16
            dst = RAW[:, slot, 0:m["n"], at:at + w]
            sp.do(lambda e, dst=dst, src=src: e.dma_start(dst, src).then_inc(s_raw[slot], 16), sig=False)
        m["tok"] = (s_raw[slot], raw_n[slot])
        state["dma"] += 1

    def split_to(i):
        while state["split"] <= min(i, len(steps) - 1):
            s = state["split"]
            st = steps[s]
            m = dmas[st["dma"]]
            slot, h, w = st["dma"] % NRAW, s % NSPLIT, st["width"]
            src = RAW[:, slot, st["j"], 0:w]
            free = pe_step.get(s - NSPLIT)
            a = act.do(lambda e: e.activation(HI[:, h, 0:w], src, ACT.Copy), m["tok"], free)
            v = dve.do(lambda e: e.tensor_tensor(LO[:, h, 0:w], src, HI[:, h, 0:w].bitcast(F32), ALU.subtract),
                       a, m["tok"], free)
            split_tok[s] = (a, v)
            state["split"] += 1
            if st["j"] == m["n"] - 1:
                issue_dma()

    KT = {}

    def kslot(i):
        return (KPA, i) if i < 16 else (KT["b"], i - 16)

    free_pairs = []
    pair_free = {}

    def take_pair():
        p = free_pairs.pop(0)
        return p, pair_free.get(p, [])

    def give(slots, tok):
        for p in sorted({s // 2 for s, _ in slots}):
            pair_free[p] = [tok]
            free_pairs.append(p)

    main = Banks([0, 2, 4])
    side = Banks([6, 7])

    def run(u, chunks, evac, sides=(), feeder=None, ends=()):
        w, nb = u["width"], (u["width"] + 511) // 512
        b0, f0 = main.take()
        b1, f1 = main.take()
        toks = [None, None]
        for i in range(u["nk"]):
            s = u["first"] + i
            while feeder is not None and len(chunks) < min(i + FEED_AHEAD, u["nk"]):
                next(feeder)
            split_to(s + LA)
            h = s % NSPLIT
            slot, ready = chunks[i]
            kt, ks = kslot(slot)
            for t, (b, f) in enumerate(((b0, f0), (b1, f1))):
                pe.wait(*split_tok[s], ready)
                if i == 0:
                    pe.wait(f)
                hi = kt[:, ks, 0, t * 128:(t + 1) * 128]
                lo = kt[:, ks, 1, t * 128:(t + 1) * 128]
                end = i == u["nk"] - 1
                for part, (l, r) in enumerate(((hi, HI), (hi, LO), (lo, HI))):
                    for j in range(nb):
                        cw = min(512, w - 512 * j)
                        o, c = PS[:, b + j, 0:cw], slice(512 * j, 512 * j + cw)
                        sig = part == 2 and j == nb - 1 and (t == 1 or end)
                        tk = pe.do(lambda e: e.matmul(o, l, r[:, h, c], start=(i == 0 and part == 0), stop=(end and part == 2)),
                                   sig=sig)
                        if sig:
                            toks[t] = tk
                if t == 1:
                    pe_step[s] = toks[1]
            for g in sides:
                next(g, None)
        for g in ends:
            finish(g)
        for t, b in enumerate((b0, b1)):
            main.done(b, evac(t, b, toks[t]))
        return toks[1]

    def finish(g):
        for _ in g:
            pass

    def feed(srcs, gain, got, ready):
        n = len(ready)
        for c in range(0, n, 2):
            bank, fr = side.take()
            pe.wait(fr)
            for q in range(2):
                for t in range(2):
                    o = PS[:, bank, q * 256 + t * 128:q * 256 + t * 128 + 128]
                    s = srcs(c + q, t)
                    tk = pe.do(lambda e, o=o, s=s: e.transpose(o, s, ID[:, :]), ready[c + q], t_id,
                               sig=(q == 1 and t == 1))
            pair, pf = take_pair()
            kt, ks = kslot(2 * pair)
            if gain is None:
                src = PS[:, bank, :].rearrange("p (a b) -> p a b", a=2)
                a = act.do(lambda e: e.activation(kt[:, ks:ks + 2, 0, :], src, ACT.Copy), tk, pf)
                v = dve.do(lambda e: e.tensor_tensor(kt[:, ks:ks + 2, 1, :], src,
                                                     kt[:, ks:ks + 2, 0, :].bitcast(F32), ALU.subtract), a, tk, pf)
            else:
                for q in range(2):
                    src = PS[:, bank, q * 256:q * 256 + 256]
                    g = par(gain, c + q, 1)
                    a = act.do(lambda e: e.activation(kt[:, ks + q, 0, :], src, ACT.Copy, scale=g), tk, pf, t_par)
                for q in range(2):
                    src = PS[:, bank, q * 256:q * 256 + 256]
                    g = par(gain, c + q, 1)
                    v = dve.do(lambda e: e.scalar_tensor_tensor(
                        out=kt[:, ks + q, 1, :], in0=src, scalar=g, in1=kt[:, ks + q, 0, :].bitcast(F32),
                        op0=ALU.mult, op1=ALU.subtract), a, tk, pf, t_par)
            side.done(bank, [a, v])
            for q in range(2):
                got.append((2 * pair + q, [a, v]))
            yield

    def feed_split(srcs, got, n, ready):
        for c in range(0, n, 2):
            pair, pf = take_pair()
            kt, ks = kslot(2 * pair)
            src = srcs(c)
            a = act.do(lambda e: e.activation(kt[:, ks:ks + 2, 0, :], src, ACT.Copy), ready[c], ready[c + 1], pf)
            v = dve.do(lambda e: e.tensor_tensor(kt[:, ks:ks + 2, 1, :], src,
                                                 kt[:, ks:ks + 2, 0, :].bitcast(F32), ALU.subtract),
                       a, ready[c], ready[c + 1], pf)
            for q in range(2):
                got.append((2 * pair + q, [a, v]))
            yield

    def inv_root(dst, ssq, n, count, eps, *tokens):
        tmp = small(n)
        a = dve.do(lambda e: e.tensor_scalar(tmp, ssq, 1.0 / count, eps, ALU.mult, ALU.add), *tokens)
        return pool.do(lambda e: e.tensor_tensor(dst, tmp, NEG5[:, 0:n], ALU.pow), a, t_n5)

    def add_small(dst, a, b, *tokens):
        return dve.do(lambda e: e.tensor_tensor(dst, a, b, ALU.add), *tokens)

    t_id = load(ID[:, :], inp["ident"])
    t_par = load(PAR[:, :], inp["params"])
    xr_tok = {}
    for c in range(4):
        t_x = load(XR[:, :, 512 * c:512 * c + 512],
                   inp["x"][:, 512 * c:512 * c + 512].rearrange("(t p) c -> p t c", p=128))
        for t in range(2):
            xr_tok[(t, c)] = t_x

    jk_tok = [None]
    JK_ = [None]

    def norm_feed(nm):
        for c in range(0, 16, 4):
            rd = [[xr_tok[(0, c // 4)], xr_tok[(1, c // 4)]]] * 4
            COLS[(nm["gain"], c)] = (COLS[nm["gain"]][0] + c, COLS[nm["gain"]][0] + c + 4)
            yield from feed(lambda i, t: XR[:, t, (c + i) * 128:(c + i + 1) * 128], (nm["gain"], c), nm["got"], rd)

    def norm_stats(nm):
        for c in range(2):
            for t in range(2):
                jk_tok[0] = act.do(lambda e: e.activation(JK_[0][:, :], XR[:, t, c * 1024:(c + 1) * 1024], ACT.Square,
                                                          accum_out=nm["part"][:, 2 * c + t:2 * c + t + 1]),
                                   xr_tok[(t, 2 * c)], xr_tok[(t, 2 * c + 1)], jk_tok[0])
                yield
        a = add_small(nm["ss"], nm["part"][:, 0:2], nm["part"][:, 2:4], jk_tok[0])
        nm["tr"] = inv_root(nm["r"], nm["ss"], 2, D, EPS, a)
        yield

    def new_norm(gain):
        nm = dict(gain=gain, part=small(4), ss=small(2), r=small(2), got=[], tr=None)
        nm["feed"], nm["stats"] = norm_feed(nm), norm_stats(nm)
        return nm

    def part_of(nm, n):
        yield
        yield
        while len(nm["got"]) < n:
            next(nm["feed"])
            yield

    w_in, w_out = inp["w_in"], inp["w_out"]
    U = {}
    U["u"] = unit([(w_in, 1536, 1024)], 0, 16)
    U["q"] = unit([(w_in, 0, 1024)], 0, 16)
    U["kv"] = unit([(w_in, 1024, 512)], 0, 16)
    U["wa"] = [unit([(w_out, 1024 * i, 1024)], 0, 8) for i in range(2)]
    U["glu"] = unit([(inp["w_glu"], 0, 1024)], 0, 8)
    U["ws"] = [unit([(w_out, 1024 * i, 1024)], 8, 8) for i in range(2)]
    nu = HID1 // 512
    U["up1"], U["dn1"] = [None] * nu, {}

    def up1(i):
        U["up1"][i] = unit([(inp["w_ff_gate"], 512 * i, 512), (inp["w_ff_up"], 512 * i, 512)], 0, 16)

    order1 = []
    for blk in range((nu + 1) // 2):
        for i in range(2 * blk, min(2 * blk + 2, nu)):
            up1(i)
            order1.append(("up", i))
        if blk:
            U["dn1"][blk - 1] = [unit([(inp["w_ff_down"], 1024 * c, 1024)], 8 * (blk - 1), 8) for c in range(2)]
            order1.append(("dn", blk - 1))
    blk = (nu + 1) // 2 - 1
    U["dn1"][blk] = [unit([(inp["w_ff_down"], 1024 * c, 1024)], 8 * blk, 2 * (HID1 // 256) - 8 * blk) for c in range(2)]
    order1.append(("dn", blk))
    wab = inp["w_in_ab"]
    U["ab"] = [unit([(wab, 1024 * c, 1024)], 0, 16) for c in (1, 3, 4, 2, 0)]
    U["oab"] = [unit([(inp["w_out_ab"], 1024 * c, 1024)], 0, 16, list(range(8, 16)) + list(range(8))) for c in range(2)]

    def ffn2_units(layer):
        ups, dns, order = [], [], []
        for b in range(HID2 // 1024):
            ups.append(unit([(inp["w_up"][layer], 1024 * b, 1024)], 0, 16))
            order.append(("up", b))
            if b:
                dns.append([unit([(inp["w_down"][layer], 1024 * c, 1024)], 8 * (b - 1), 8) for c in range(2)])
                order.append(("dn", b - 1))
        b = HID2 // 1024 - 1
        dns.append([unit([(inp["w_down"][layer], 1024 * c, 1024)], 8 * b, 8) for c in range(2)])
        order.append(("dn", b))
        return ups, dns, order

    F2 = [ffn2_units(0)]
    U["qkv"] = [[unit([(inp["w_qkv"], 2048 * p + 1024 * hf, 1024)], 0, 16) for p in range(3)] for hf in range(2)]
    U["wo"] = [[unit([(inp["w_o"], 1024 * c, 1024)], 8 * hf, 8) for c in range(2)] for hf in range(2)]
    F2.append(ffn2_units(1))

    for _ in range(NRAW):
        issue_dma()

    free_pairs.extend(range(8))

    NEG5 = sb([128, 48], name="NEG5")
    t_n5 = pool.do(lambda e: e.memset(NEG5[:, :], -0.5))
    kb_region = Region(keep.at)
    ph = Region(keep.at + 32768)
    u_sb = ACC[:, 0, :].rearrange("p (t c) -> p t c", t=2)
    uT = ACC[:, 1, :].rearrange("p (k c) -> p k c", k=8)
    yT = u_sb.rearrange("p t c -> p (t c)").rearrange("p (k c) -> p k c", k=8)
    WK = [sb([128, 512], stack=kb_region, name="WK") for _ in range(16)]
    q_sb = sb([128, 2, 1024], stack=ph, name="q_sb")
    kv_sb = sb([128, 2, 512], stack=ph, name="kv_sb")
    upper = Region(kpa_at + 16384)
    qT = sb([128, 8, 256], stack=upper, name="qT")
    kT = sb([128, 4, 256], stack=upper, name="kT")
    KD = sb([128, 2, 4, 128], stack=upper, name="KD")
    BL = sb([128, 2, 8, 128], stack=ph, name="BL")
    CL = sb([128, 2, STATE_TILES, 32], stack=ph, name="CL")
    JK = sb([128, 1024], stack=ph, name="JK")
    BT = sb([128, 4, 384], stack=ph, name="BT")
    TAU = sb([128, 256], stack=ph, name="TAU")
    SP_ = sb([128, 16, 32], stack=ph, name="SPR")

    t_tau = load(TAU[:, :], inp["tau"])
    t_cl = load(CL[:, :, :, :].rearrange("p a b c -> p (a b c)"), inp["ssm_c"])

    JK_[0] = JK
    nm1 = new_norm("ln1")
    xT = nm1["got"]

    def to_sb(dst, nm):
        toks = [None, None]

        def evac(t, b, tok):
            d = dst(t)
            w = d.shape[-1]
            src = PS[:, b:b + (w // 512), :].rearrange("p a b -> p (a b)")
            toks[t] = act.do(lambda e: e.activation(d, src, ACT.Copy, scale=nm["r"][:, t:t + 1]), tok, nm["tr"])
            return [toks[t]]
        evac.toks = toks
        return evac

    t_qf = t_wv = t_w = t_hp = HP = mag = qf = s_w = None
    t_xb, t_bl = [], [None, None]

    def prep():
        nonlocal t_qf, t_wv, t_w, t_hp, HP, mag, qf, s_w, t_cl
        sp_i = [0]

        def spt():
            sp_i[0] += 1
            return SP_[:, sp_i[0] - 1, :]

        bn_re, bn_im = WK[0], WK[1]
        t_bn = [load(bn_re[:, :], inp["ssm_b"][0]), load(bn_im[:, :], inp["ssm_b"][1])]
        E_ = sb([128, 1], stack=ph, name="EB")
        HP = sb([128, 1], stack=ph, name="HP")
        EB = E_[:, 0:1]
        t_e = pool.do(lambda e: e.memset(EB, float(np.e)))
        t_hp = pool.do(lambda e: e.memset(HP[:, :], float(np.pi / 2)))
        mag, qf, fre, fim, dt_, ang, v1, v2, v3, v4, v5, v6 = [spt() for _ in range(12)]
        are, aim = par("a_re"), par("a_im")
        t_cl = dve.do(lambda e: e.tensor_scalar(CL[:, 1, :, :], CL[:, 1, :, :], -1.0, None, ALU.mult), t_cl)
        eb = bass.AP(E_[:, 0:1].tensor, E_[:, 0:1].offset, [list(E_[:, 0:1].ap[0]), [0, 32]])
        a = pool.do(lambda e: e.tensor_tensor(dt_, eb, par("ldt"), ALU.pow), t_e, t_par)
        a = pool.do(lambda e: e.tensor_tensor(v1, are, dt_, ALU.mult), a)
        p_ang = pool.do(lambda e: e.tensor_tensor(ang, aim, dt_, ALU.mult), a)
        p_mag = pool.do(lambda e: e.tensor_tensor(mag, eb, v1, ALU.pow), p_ang)
        inv2pi = 1.0 / TWO_PI
        c1 = 6.28125
        c2 = 0.0019350051879882812
        c3 = TWO_PI - c1 - c2
        v = dve.do(lambda e: e.tensor_scalar(v2, ang, inv2pi, None, ALU.mult), p_ang)
        v = dve.do(lambda e: e.tensor_scalar(v3, v2, MAGIC, -MAGIC, ALU.add, ALU.add), v)
        v = dve.do(lambda e: e.scalar_tensor_tensor(out=v4, in0=v3, scalar=-c1, in1=ang, op0=ALU.mult, op1=ALU.add), v)
        v = dve.do(lambda e: e.scalar_tensor_tensor(out=v5, in0=v3, scalar=-c2, in1=v4, op0=ALU.mult, op1=ALU.add), v)
        v = dve.do(lambda e: e.scalar_tensor_tensor(out=v4, in0=v3, scalar=-c3, in1=v5, op0=ALU.mult, op1=ALU.add), v)
        v = dve.do(lambda e: e.tensor_scalar(v5, v4, 3.1415925, -3.1415925, ALU.min, ALU.max), v)
        t_qf = dve.do(lambda e: e.tensor_scalar(qf, v4, inv2pi, None, ALU.mult), v)
        a = act.do(lambda e: e.activation(v6, v5, ACT.Sin), v)
        a = act.do(lambda e: e.activation(v3, v5, ACT.Sin, scale=0.5), t_qf)
        yield
        v = dve.do(lambda e: e.scalar_tensor_tensor(out=v1, in0=v3, scalar=-2.0, in1=v3, op0=ALU.mult, op1=ALU.mult), a, p_mag)
        v = dve.do(lambda e: e.tensor_scalar(v2, v1, 1.0, None, ALU.add), v)
        v = dve.do(lambda e: e.scalar_tensor_tensor(out=v3, in0=mag, scalar=-1.0, in1=v2, op0=ALU.add, op1=ALU.mult), v)
        v = dve.do(lambda e: e.tensor_tensor(v2, v3, v1, ALU.add), v)
        v = dve.do(lambda e: e.tensor_tensor(v4, mag, v6, ALU.mult), v)
        yield
        v = dve.do(lambda e: e.tensor_tensor(v1, are, are, ALU.mult), v)
        v = dve.do(lambda e: e.tensor_tensor(v3, aim, aim, ALU.mult), v)
        v = dve.do(lambda e: e.tensor_tensor(v5, v1, v3, ALU.add), v)
        v = dve.do(lambda e: e.reciprocal(v1, v5), v)
        v = dve.do(lambda e: e.tensor_tensor(v3, v2, are, ALU.mult), v)
        v = dve.do(lambda e: e.tensor_tensor(v5, v4, aim, ALU.mult), v)
        v = dve.do(lambda e: e.tensor_tensor(v6, v3, v5, ALU.add), v)
        v = dve.do(lambda e: e.tensor_tensor(fre, v6, v1, ALU.mult), v)
        v = dve.do(lambda e: e.tensor_tensor(v3, v4, are, ALU.mult), v)
        v = dve.do(lambda e: e.tensor_tensor(v5, v2, aim, ALU.mult), v)
        v = dve.do(lambda e: e.tensor_tensor(v6, v3, v5, ALU.subtract), v)
        t_f = dve.do(lambda e: e.tensor_tensor(fim, v6, v1, ALU.mult), v)

        yield
        def b3(t):
            return t[:, :].rearrange("p (j c) -> p j c", c=16)

        frb, fib = bcast(fre, 2, 16), bcast(fim, 2, 16)
        T1, T2 = WK[2], WK[3]
        XB = [(WK[4], WK[5]), (WK[6], WK[7])]
        z = [dve.do(lambda e, w=w: e.memset(w[:, :], 0.0)) for pr in XB for w in pr]
        TS = WK[8]
        for part, (fa, fb, op) in enumerate(((frb, fib, ALU.subtract), (fib, frb, ALU.add))):
            v = dve.do(lambda e: e.tensor_tensor(b3(T1), b3(bn_re), fa, ALU.mult), t_bn, t_f)
            v = dve.do(lambda e: e.tensor_tensor(b3(T2), b3(bn_im), fb, ALU.mult), v)
            v = dve.do(lambda e: e.tensor_tensor(TS[:, :], T1[:, :], T2[:, :], op), v)
            for hf in range(2):
                dst = XB[part][hf]
                for g in range(2):
                    o = dst[64 * g:64 * g + 64, :].rearrange("p (j c) -> p j c", c=32)[:, :, 16 * g:16 * g + 16]
                    s = TS[64 * g:64 * g + 64, :].rearrange("p (j c) -> p j c", c=16)[:, 16 * hf:16 * hf + 16, :]
                    w = dve.do(lambda e: e.tensor_copy(o, s), v, z)
            v = w
            t_xb.append(w)
            t_f = w
            yield
        yield
        for part in range(2):
            for hf in range(2):
                bank, fr = side.take()
                for q in range(4):
                    o = PS[:, bank, q * 128:(q + 1) * 128]
                    s = XB[part][hf][:, q * 128:(q + 1) * 128]
                    tk = pe.do(lambda e, o=o, s=s: e.transpose(o, s, ID[:, :]), fr, t_xb[part], t_id, sig=(q == 3))
                d = BL[:, part, 4 * hf:4 * hf + 4, :].rearrange("p a b -> p (a b)")
                a = act.do(lambda e: e.activation(d, PS[:, bank, :], ACT.Copy), tk)
                side.done(bank, [a])
                t_bl[part] = a
                yield

        yield
        RB, OH = WK[9][0:33, 0:16], WK[10][0:33, 0:383]
        t_rb = load(RB[0:32, :], inp["rel_bias"])
        t_rb2 = pool.do(lambda e: e.memset(RB[32:33, :], 1.0))
        t_oh = load(OH, inp["onehot"])
        WV = WK[11]
        bank, fr = side.take()
        t_wv = tk = pe.do(lambda e: e.matmul(PS[0:16, bank, 0:383], RB, OH, start=True, stop=True), fr, t_rb, t_rb2, t_oh)
        a = act.do(lambda e: e.activation(WV[0:16, 0:383], PS[0:16, bank, 0:383], ACT.Copy), tk)
        side.done(bank, [a])
        s_w = sem("bias_written")
        sp.wait(a)
        sp.do(lambda e: e.dma_start(scratch[:, :, 0:383], bcast(WV[0:16, 0:383], 1, 128)).then_inc(s_w, 16), sig=False)
        t_w = (s_w, 16)
        yield

    ev = to_sb(lambda t: u_sb[:, t, :], nm1)
    pr = prep()
    run(U["u"], xT, ev, [pr, nm1["stats"]], nm1["feed"], [pr, nm1["stats"]])
    t_u = ev.toks
    t_uT = []

    def u_turn():
        for c in range(0, 8, 2):
            bank, fr = side.take()
            for q in range(2):
                for t in range(2):
                    o = PS[:, bank, q * 256 + t * 128:q * 256 + t * 128 + 128]
                    s = u_sb[:, t, (c + q) * 128:(c + q + 1) * 128]
                    tk = pe.do(lambda e, o=o, s=s: e.transpose(o, s, ID[:, :]), fr, t_u[t], sig=(q == 1 and t == 1))
            d = uT[:, c:c + 2, :].rearrange("p a b -> p (a b)")
            a = act.do(lambda e: e.activation(d, PS[:, bank, :], ACT.Copy), tk)
            side.done(bank, [a])
            t_uT.extend([a, a])
            yield

    t_y = {}

    def pair_view(b0, b1, c):
        a = PS[:, b0, c:c + 256]
        return bass.AP(a.tensor, a.offset, [list(a.ap[0]), [(b1 - b0) * 512, 2], [1, 256]])

    y_half = {}

    def ssm_side(par_):
        if par_ == 0:
            yield from u_turn()
        else:
            for _ in range(6):
                yield
        w = WK[8 * par_:8 * par_ + 8]
        phi, rnd, sn, cs, g_re, g_im, m1, m2 = w
        old = None

        def t3(x):
            return x[:, :].rearrange("p (j c) -> p j c", j=2)

        for b in range(par_, 16, 2):
            kc, hh = b // 2, b % 2
            j0 = 2 * b
            for i in range(2):
                a = act.do(lambda e: e.activation(phi[:, 256 * i:256 * i + 256], TAU[:, :], ACT.Copy,
                                                  scale=qf[:, j0 + i:j0 + i + 1]), t_qf, t_tau, t_xb, t_bl, t_wv, t_w, old)
            yield
            p = a
            v = dve.do(lambda e: e.tensor_scalar(rnd[:, :], phi[:, :], MAGIC, -MAGIC, ALU.add, ALU.add), p)
            p = pool.do(lambda e: e.tensor_tensor(sn[:, :], phi[:, :], rnd[:, :], ALU.subtract), v)
            yield
            a = act.do(lambda e: e.activation(phi[:, :], sn[:, :], ACT.Abs), p)
            a1 = act.do(lambda e: e.activation(rnd[:, :], sn[:, :], ACT.Sin, scale=6.283185), p)
            a2 = act.do(lambda e: e.activation(cs[:, :], phi[:, :], ACT.Sin, scale=-6.283185, bias=HP[:, 0:1]), a, t_hp)
            sn2 = rnd
            yield
            b0, f0 = side.take()
            b1, f1 = side.take()
            if b0 > b1:
                b0, f0, b1, f1 = b1, f1, b0, f0
            for part in range(2):
                for i, (bk, ff) in enumerate(((b0, f0), (b1, f1))):
                    r0 = 64 * hh + 32 * i
                    l = BL[r0:r0 + 32, part, kc, :]
                    rr = uT[r0:r0 + 32, kc, :]
                    o = PS[:, bk, part * 256:(part + 1) * 256]
                    tk = pe.do(lambda e: e.matmul(o, l, rr, start=True, stop=True), ff, t_bl[part], t_uT[kc])
            ure, uim = pair_view(b0, b1, 0), pair_view(b0, b1, 256)
            v1_ = dve.do(lambda e: e.tensor_tensor(t3(m1), t3(cs), ure, ALU.mult), a2, a1, tk)
            v2_ = dve.do(lambda e: e.tensor_tensor(t3(m2), t3(sn2), uim, ALU.mult))
            p1 = pool.do(lambda e: e.tensor_tensor(m1[:, :], m1[:, :], m2[:, :], ALU.add), v2_)
            v3_ = dve.do(lambda e: e.tensor_tensor(t3(phi), t3(cs), uim, ALU.mult))
            v4_ = dve.do(lambda e: e.tensor_tensor(t3(sn), t3(sn2), ure, ALU.mult))
            side.done(b0, [v4_])
            side.done(b1, [v4_])
            p2 = pool.do(lambda e: e.tensor_tensor(m2[:, :], phi[:, :], sn[:, :], ALU.subtract), v4_, p1)
            yield
            for src, dst, pp in ((m1, g_re, p1), (m2, g_im, p2)):
                for i in range(2):
                    dcy = bass.AP(mag.tensor, mag[:, j0 + i:j0 + i + 1].offset, [list(mag.ap[0]), [0, 256]])
                    c = slice(256 * i, 256 * i + 256)
                    v = dve.do(lambda e: e.tensor_tensor_scan(dst[:, c], dcy, src[:, c], 0.0, ALU.mult, ALU.add), pp)
            P1, P2, P3, P4 = m1, phi, sn, m2
            pd = pool.do(lambda e: e.tensor_tensor(P4[:, :], cs[:, :], g_im[:, :], ALU.mult), v)
            va = dve.do(lambda e: e.tensor_tensor(P1[:, :], cs[:, :], g_re[:, :], ALU.mult), v)
            vb = dve.do(lambda e: e.scalar_tensor_tensor(out=P2[:, :], in0=g_im[:, :], scalar=-1.0, in1=sn2[:, :],
                                                         op0=ALU.mult, op1=ALU.mult), p2)
            vc = dve.do(lambda e: e.tensor_tensor(P3[:, :], sn2[:, :], g_re[:, :], ALU.mult))
            yield
            by, fy = side.take()
            for n, (P, part) in enumerate(((P1, 0), (P2, 0), (P3, 1), (P4, 1))):
                for i in range(2):
                    r0 = 64 * hh + 32 * i
                    o = PS[r0:r0 + 32, by, 0:256]
                    c = slice(256 * i, 256 * i + 256)
                    l = CL[:, part, j0 + i, :]
                    tk = pe.do(lambda e: e.matmul(o, l, P[:, c], start=(n == 0), stop=(n == 3)),
                               fy, va, vb, vc, pd, t_cl, sig=(i == 1 and n == 3))
            old = [tk]
            yield
            h0 = slice(64 * hh, 64 * hh + 64)
            yb = slice(256 * (kc % 4), 256 * (kc % 4) + 256)
            v = dve.do(lambda e: e.scalar_tensor_tensor(out=JK[h0, yb], in0=uT[h0, kc, :], scalar=par("d", kc, 1)[h0, :],
                                                        in1=PS[h0, by, 0:256], op0=ALU.mult, op1=ALU.add),
                       tk, t_par, jk_tok[0], t_uT[7], t_y.get(kc - 4))
            side.done(by, [v])
            y_half[b] = v
            if (b ^ 1) in y_half:
                t_y[kc] = act.do(lambda e: e.activation(yT[:, kc, :], JK[:, yb], ACT.Gelu_apprx_tanh),
                                 y_half[b], y_half[b ^ 1])
            yield

    main.banks, main.at = [0, 2], 0
    side.free[4] = main.free[4]
    side.free[5] = main.free[4]
    side.banks = [4, 5, 6, 7]
    for b in (0, 1, 2, 3):
        side.free.setdefault(b, [])
    S0, S1 = ssm_side(0), ssm_side(1)
    evq = to_sb(lambda t: q_sb[:, t, :], nm1)
    run(U["q"], xT, evq, [S0, S1])
    evk = to_sb(lambda t: kv_sb[:, t, :], nm1)
    tl = run(U["kv"], xT, evk, [S0, S1])
    give(xT, tl)

    sqs = small(32)
    rq = small(32)
    sks = small(8)
    rk = small(8)
    t_q, t_k = evq.toks, evk.toks
    qn, kn = [None, None], [None, None]
    def make_stats():
        n = small(12), small(8), small(8), small(8), small(8), small(8), small(8)
        return n

    def attn_buffers(region_l, region_p, stats=None):
        return dict(LG=sb([128, 4, 384], stack=region_l, name="LG"), PT=sb([128, 4, 384], stack=region_p, name="PT"),
                    stats=stats or make_stats(), pt=[None] * 4, o=[None] * 4, st=[])

    lower = Region(kpa_at)
    AB = [attn_buffers(ph, ph), attn_buffers(lower, lower)]
    SQ = AB[0]["PT"][:, :, :].rearrange("p a b -> p (a b)")[:, 0:1024]
    AB[0]["BT"], AB[1]["BT"] = BT, sb([128, 4, 384], stack=ph, name="BT")

    def heads(ap, n):
        return ap.rearrange("p (h d) -> p h d", h=n)

    pv_ = None
    for t in range(2):
        a = act.do(lambda e: e.activation(SQ[:, :], q_sb[:, t, :], ACT.Square), t_q[t], pv_)
        v = dve.do(lambda e: e.tensor_reduce(sqs[:, 16 * t:16 * t + 16], heads(SQ[:, :], 16), X, ALU.add), a)
        a = act.do(lambda e: e.activation(SQ[:, 0:256], kv_sb[:, t, 0:256], ACT.Square), t_k[t], v)
        pv_ = dve.do(lambda e: e.tensor_reduce(sks[:, 4 * t:4 * t + 4], heads(SQ[:, 0:256], 4), X, ALU.add), a)
    p1 = inv_root(rq, sqs, 32, 64, EPS, pv_)
    p2 = inv_root(rk, sks, 8, 64, EPS, pv_)
    for t in range(2):
        qn[t] = dve.do(lambda e: e.tensor_tensor(heads(q_sb[:, t, :], 16), heads(q_sb[:, t, :], 16),
                                                 bcast(rq[:, 16 * t:16 * t + 16], 2, 64), ALU.mult), p1, t_q[t])
        for dd in range(2):
            kn[t] = dve.do(lambda e: e.tensor_tensor(KD[:, t, :, 64 * dd:64 * dd + 64], heads(kv_sb[:, t, 0:256], 4),
                                                     bcast(rk[:, 4 * t:4 * t + 4], 2, 64), ALU.mult), p2, t_k[t])
    t_qT, t_kT = {}, {}

    def turn(src, dst, c, gain, *tokens):
        bank, fr = side.take()
        for q in range(2):
            for t in range(2):
                o = PS[:, bank, q * 256 + t * 128:q * 256 + t * 128 + 128]
                s = src(c + q, t)
                tk = pe.do(lambda e, o=o, s=s: e.transpose(o, s, ID[:, :]), fr, *tokens, sig=(q == 1 and t == 1))
        d = dst[:, c:c + 2, :].rearrange("p a b -> p (a b)")
        if gain is None:
            a = act.do(lambda e: e.activation(d, PS[:, bank, :], ACT.Copy), tk, *tokens)
        else:
            a = act.do(lambda e: e.activation(d, PS[:, bank, :], ACT.Copy, scale=gain), tk, *tokens)
        side.done(bank, [a])
        return a

    def attn_prep():
        for c in (0, 2):
            t_kT[c] = t_kT[c + 1] = turn(lambda cc, t: KD[:, t, cc, :], kT, c, par("kg"), kn, t_par)
            yield
        for c in range(0, 8, 2):
            t_qT[c] = t_qT[c + 1] = turn(lambda cc, t: q_sb[:, t, cc * 128:(cc + 1) * 128], qT, c, par("qg"), qn, t_par)
            yield

    def attn_group(n, q_of, k_of, v_of, dv, scale, mask, tmask, sinks, write, B, tr):
        LG, PT = B["LG"], B["PT"]
        mx, mm, ng, sm, sk, den, rc = B["stats"]
        tS = []
        for h in range(4):
            bank, fr = side.take()
            q, k, tq = q_of(h), k_of(h), tr[h]
            pe.do(lambda e: e.matmul(PS[:, bank, 0:128], q[:, 0:128], k[:, 0:128], start=True, stop=True), fr, tq, sig=False)
            tk = pe.do(lambda e: e.matmul(PS[:, bank, 128:384], q[:, 128:256], k, start=True, stop=True))
            mk = mask(h)
            v = dve.do(lambda e: e.scalar_tensor_tensor(out=LG[:, h, :], in0=PS[:, bank, 0:384], scalar=scale, in1=mk,
                                                        op0=ALU.mult, op1=ALU.add), tk, tmask, B["pt"][h])
            side.done(bank, [v])
            tS.append(v)
            if h % 2:
                yield
        mx3 = mx.rearrange("p (h s) -> p h s", s=3)
        mm2 = mm.rearrange("p (h s) -> p h s", s=2)
        v = dve.do(lambda e: e.tensor_reduce(mx3, LG[:, :, :].rearrange("p h (s c) -> p h s c", s=3), X, ALU.max),
                   tS, B["st"])
        v = dve.do(lambda e: e.tensor_tensor(mm2[:, :, 1], mx3[:, :, 1], mx3[:, :, 2], ALU.max), v)
        if sinks is not None:
            v = dve.do(lambda e: e.tensor_tensor(mm2[:, :, 1], mm2[:, :, 1], sinks, ALU.max), v)
            v = dve.do(lambda e: e.tensor_tensor(mm2[:, :, 0], mx3[:, :, 0], sinks, ALU.max), v)
        else:
            v = dve.do(lambda e: e.tensor_copy(mm2[:, :, 0], mx3[:, :, 0]), v)
        vn = dve.do(lambda e: e.tensor_scalar(ng, mm, -1.0, None, ALU.mult), v)
        if sinks is not None:
            v = dve.do(lambda e: e.tensor_tensor(sk.rearrange("p (h s) -> p h s", s=2), bcast(sinks, 2, 2),
                                                 ng.rearrange("p (h s) -> p h s", s=2), ALU.add), vn)
            ask = act.do(lambda e: e.activation(sk, sk, ACT.Exp), v)
        yield
        ta = []
        for h in range(4):
            for s, (c0, c1_) in enumerate(((0, 128), (128, 384))):
                a = act.do(lambda e: e.activation(LG[:, h, c0:c1_], LG[:, h, c0:c1_], ACT.Exp,
                                                  bias=ng[:, 2 * h + s:2 * h + s + 1],
                                                  accum_out=sm[:, 2 * h + s:2 * h + s + 1]), vn)
            ta.append(a)
            if h == 1:
                yield
        if sinks is not None:
            v = dve.do(lambda e: e.tensor_tensor(den, sm, sk, ALU.add), ta, ask)
        else:
            v = dve.do(lambda e: e.tensor_copy(den, sm), ta)
        tr_ = dve.do(lambda e: e.reciprocal(rc, den), v)
        yield
        per = 512 // (2 * dv)
        for h0 in (0, 2):
            cp = []
            for h in (h0, h0 + 1):
                bank, fr = side.take()
                for q in range(3):
                    o, sr = PS[:, bank, q * 128:(q + 1) * 128], LG[:, h, q * 128:(q + 1) * 128]
                    tk = pe.do(lambda e: e.transpose(o, sr, ID[:, :]), fr, ta[h], sig=(q == 2))
                B["pt"][h] = tk
                if h % 2:
                    c = dve.do(lambda e: e.tensor_copy(PT[:, h, :], PS[:, bank, 0:384]), tk, B["o"][h])
                else:
                    c = act.do(lambda e: e.activation(PT[:, h, :], PS[:, bank, 0:384], ACT.Copy), tk, B["o"][h])
                side.done(bank, [c])
                cp.append(c)
            yield
            if h0 % per == 0:
                ob, fo = side.take()
                pe.wait(fo)
            for h in (h0, h0 + 1):
                x0 = (h % per) * 2 * dv
                va, vb = v_of(h, 0), v_of(h, 1)
                pe.do(lambda e: e.matmul(PS[:, ob, x0:x0 + dv], PT[:, h, 0:128], va, start=True, stop=True),
                      cp[h - h0], sig=False)
                pe.do(lambda e: e.matmul(PS[:, ob, x0 + dv:x0 + 2 * dv], PT[:, h, 128:256], va, start=True, stop=False),
                      sig=False)
                tk = pe.do(lambda e: e.matmul(PS[:, ob, x0 + dv:x0 + 2 * dv], PT[:, h, 256:384], vb, start=False, stop=True))
                B["o"][h] = tk
            if h % per == per - 1:
                for t in range(2):
                    src = PS[:, ob, :].rearrange("p (h t d) -> p t h d", t=2, d=dv)[:, t]
                    r = rc.rearrange("p (h s) -> p s h", s=2)[:, t, h - per + 1:h + 1]
                    w = write(t, h - per + 1, per, src, bcast(r, 2, dv), tk, tr_)
                side.done(ob, [w])
            yield
        B["st"] = [w]


    t_att = {}

    def load_bias(g, BT, *tokens):
        s = sem(f"bias{g}")
        sp.wait(t_w, *tokens)
        for h in range(4):
            for c0, n, off in ((0, 128, 128), (128, 256, 0)):
                src = bass.AP(scratch.tensor, (4 * g + h) * 128 * 384 + 127 + off, [[383, 128], [1, n]])
                dst = BT[:, h, c0:c0 + n]
                sp.do(lambda e, src=src, dst=dst: e.dma_start(dst, src).then_inc(s, 16), sig=False)
        return (s, 128)

    def attn1(which):
        B = AB[which]
        if which == 0:
            yield from attn_prep()
        else:
            for _ in range(7):
                yield
        for h in range(4):
            B["o"][h] = p1
        for g in (which, which + 2):
            tb = load_bias(g, B["BT"], list(B["st"]))

            def write(t, h0, per, src, r, tk, trr):
                c0 = (4 * g + h0) * 64
                d = heads(q_sb[:, t, c0:c0 + per * 64], per)
                t_att[(t, g)] = dve.do(lambda e: e.tensor_tensor(d, src, r, ALU.mult), tk, trr, list(t_qT.values()))
                return t_att[(t, g)]

            def q_of(h):
                b = 64 * (h % 2)
                return qT[b:b + 64, 2 * g + h // 2, :]

            def k_of(h):
                b = 64 * (h % 2)
                return kT[b:b + 64, g, :]
            yield from attn_group(g, q_of, k_of, lambda h, t: kv_sb[:, t, 256 + 64 * g:320 + 64 * g], 64, 0.125,
                                  lambda h: B["BT"][:, h, :], tb, par("sinks", 4 * g, 4), write, B,
                                  [[t_qT[2 * g + h // 2], t_kT[g], t_k] for h in range(4)])

    A0, A1 = attn1(0), attn1(1)

    def drive(first, *others):
        for _ in first:
            for g in others:
                next(g, None)

    for b in (0, 1, 2, 3):
        side.free[b] = list(main.free[b // 2 * 2])
    side.banks = [4, 5, 6, 7, 0, 1, 2, 3]
    drive(A0, A1, S0, S1)
    finish(A1)
    asq, rA = small(2), small(2)
    for t in range(2):
        a = act.do(lambda e: e.activation(SQ[:, :], q_sb[:, t, :], ACT.Square, accum_out=asq[:, t:t + 1]),
                   [t_att[(t, g)] for g in range(4)], a)
    t_rA = inv_root(rA, asq, 2, 1024, EPS, a)
    oT = []
    gate = all_done()
    for p in range(4):
        pair_free[p] = gate
    finish(feed(lambda c, t: q_sb[:, t, c * 128:(c + 1) * 128], "attn_g", oT,
                [[t_att[(0, c // 2)], t_att[(1, c // 2)]] for c in range(8)]))
    def add_x(c, r, tr):
        def evac(t, b, tok):
            d = XR[:, t, c * 1024:(c + 1) * 1024]
            src = PS[:, b:b + 2, :].rearrange("p a b -> p (a b)")
            if r is None:
                v = dve.do(lambda e: e.tensor_tensor(d, src, d, ALU.add), tok, xr_tok[(t, 2 * c)], xr_tok[(t, 2 * c + 1)])
            else:
                v = dve.do(lambda e: e.scalar_tensor_tensor(out=d, in0=src, scalar=r[:, t:t + 1], in1=d,
                                                            op0=ALU.mult, op1=ALU.add), tok, tr, xr_tok[(t, 2 * c)], xr_tok[(t, 2 * c + 1)])
            xr_tok[(t, 2 * c)] = xr_tok[(t, 2 * c + 1)] = v
            return [v]
        return evac

    side.banks = [4, 5, 6, 7]
    assert not side.held & {0, 1, 2, 3}
    main.free[0] = side.free[0] + side.free[1]
    main.free[2] = side.free[2] + side.free[3]
    for c in range(2):
        tl = run(U["wa"][c], oT, add_x(c, rA, t_rA), [S0, S1])
    give(oT, tl)
    drive(S0, S1)
    finish(S1)
    t_y = [t_y[c] for c in range(8)]

    gate = all_done()
    kb_region.clear()
    KT["b"] = sb([128, 16, 2, 256], F32R, stack=kb_region, name="KPB")
    for p in range(4, 8):
        pair_free[p] = gate
    for p in range(8, 16):
        pair_free[p] = gate
        free_pairs.append(p)

    yk = []
    finish(feed_split(lambda c: yT[:, c:c + 2, :], yk, 8, t_y))
    ys = q_sb
    t_ys = [None, None]
    t_sg = {}

    def ev_glu(t, b, tok):
        src = PS[:, b:b + 2, :].rearrange("p a b -> p (a b)")
        t_sg[t] = act.do(lambda e: e.activation(ys[:, t, :], src, ACT.Sigmoid), tok, [x[1] for x in oT], pe.last())
        return [t_sg[t]]

    tl = run(U["glu"], yk, ev_glu)
    give(yk, tl)
    for t in range(2):
        for hf in range(2):
            bank, fr = side.take()
            for q in range(4):
                c = 4 * hf + q
                o, s = PS[:, bank, q * 128:(q + 1) * 128], yT[:, c, t * 128:(t + 1) * 128]
                tk = pe.do(lambda e, o=o, s=s: e.transpose(o, s, ID[:, :]), fr, t_y, sig=(q == 3))
            d = ys[:, t, 512 * hf:512 * hf + 512]
            t_ys[t] = dve.do(lambda e: e.tensor_tensor(d, d, PS[:, bank, :], ALU.mult), tk, t_sg[t])
            side.done(bank, [t_ys[t]])
    gsq, rS = small(2), small(2)
    for t in range(2):
        a = act.do(lambda e: e.activation(SQ[:, :], ys[:, t, :], ACT.Square, accum_out=gsq[:, t:t + 1]), t_ys[t], a)
    t_rS = inv_root(rS, gsq, 2, 1024, EPS, a)
    sT = []
    finish(feed(lambda c, t: ys[:, t, c * 128:(c + 1) * 128], "ssm_g", sT, [t_ys] * 8))

    side.banks = [6, 7]
    main.banks = [0, 2, 4]
    main.at = 0
    main.free[4] = side.free[4] + side.free[5]

    def sq_part(src, t, dst, jk, *tokens):
        return act.do(lambda e: e.activation(jk, src, ACT.Square, accum_out=dst), *tokens)

    nm2 = new_norm("ln2")
    run(U["ws"][0], sT, add_x(0, rS, t_rS))
    tl = run(U["ws"][1], sT, add_x(1, rS, t_rS), [part_of(nm2, 8)])
    give(sT, tl)

    def phase():
        g = all_done()
        for e in (pe, act, dve, pool, sp):
            e.wait(*g)
        ph.clear()

    phase()
    JK_[0] = sb([128, 1024], stack=ph, name="JK")
    HS = [sb([128, 2, 1024], stack=ph, name="HS") for _ in range(2)]
    SG = [sb([128, 512], stack=ph, name="SG") for _ in range(2)]
    hs_read = [None, None]
    sg_read = [None, None]
    hid = {}

    def up1_run(i, sides):
        H, half = HS[(i // 2) % 2], i % 2
        tk_h = [None, None]

        def evac(t, b, tok):
            d = H[:, t, 512 * half:512 * half + 512]
            a = act.do(lambda e: e.activation(SG[t][:, :], PS[:, b, :], ACT.Silu, scale=nm2["r"][:, t:t + 1]),
                       tok, nm2["tr"], sg_read[t])
            tk_h[t] = sg_read[t] = dve.do(lambda e: e.scalar_tensor_tensor(
                out=d, in0=PS[:, b + 1, :], scalar=nm2["r"][:, t:t + 1], in1=SG[t][:, :], op0=ALU.mult, op1=ALU.mult),
                tok, a, nm2["tr"], hs_read[(i // 2) % 2])
            return [a, tk_h[t]]
        if i == 0:
            run(U["up1"][i], nm2["got"], evac, [nm2["stats"]], nm2["feed"], [nm2["stats"]])
        else:
            run(U["up1"][i], nm2["got"], evac, sides)
        return H, half, tk_h

    pend = []
    for kind, i in order1:
        if kind == "up":
            H, half, tk_h = up1_run(i, pend)
            for g in pend:
                finish(g)
            got = hid.setdefault(i // 2, [])

            def g_(H=H, half=half, tk_h=tk_h, got=got, i=i):
                yield
                yield
                yield from feed(lambda c, t: H[:, t, 512 * half + c * 128:512 * half + (c + 1) * 128], None, got, [tk_h] * 4)
                hs_read[(i // 2) % 2] = pe.last()
            pend = [g_()]
            if i == nu - 1:
                give(nm2["got"], pe.last())
        else:
            lastb = i == (nu + 1) // 2 - 1
            if lastb:
                for g in pend:
                    finish(g)
                pend = []
                nm3 = new_norm("pre0")
            for c in range(2):
                tl = run(U["dn1"][i][c], hid[i], add_x(c, None, None), pend)
                for g in pend:
                    finish(g)
                pend = []
                if lastb and c == 0:
                    pend = [part_of(nm3, 8)]
            give(hid[i], tl)

    phase()
    JK_[0] = sb([128, 1024], stack=ph, name="JK")
    AV = sb([128, 2, 1024], stack=ph, name="AV")
    GC = sb([128, 2, 1024], stack=ph, name="GC")
    GB = sb([128, 2, 1024], stack=ph, name="GB")
    ZT = sb([128, 8, 258], stack=ph, name="ZT")
    WS = sb([128, 8, 128], stack=ph, name="WS")
    CM = sb([128, 128], stack=ph, name="CM")
    CV = [sb([128, 256], stack=ph, name="CV") for _ in range(3)]
    BO = sb([128, 2, 256], stack=ph, name="BO")
    t_ws = load(WS[:, :, :], inp["w_spatial"].rearrange("s (g t) -> s g t", g=8))
    t_cm = load(CM[:, :], inp["causal"])
    t_wm = dve.do(lambda e: e.tensor_tensor(WS[:, :, :], WS[:, :, :], bcast(CM[:, :], 1, 8), ALU.mult), t_ws, t_cm)
    t_zz = dve.do(lambda e: e.memset(ZT[:, :, 0:2], 0.0))
    mu2, vs2, rv2 = small(2), small(2), small(2)
    t_vn = [None, None]
    rr = nm3["r"]

    def flat2(b):
        return PS[:, b:b + 2, :].rearrange("p a b -> p (a b)")

    def ev_av(t, b, tok):
        a0 = act.do(lambda e: e.activation(AV[:, t, :], flat2(b), ACT.Gelu_apprx_tanh, scale=rr[:, t:t + 1],
                                           accum_out=mu2[:, t:t + 1]), tok, nm3["tr"])
        v = dve.do(lambda e: e.tensor_scalar(mu2[:, t:t + 1], mu2[:, t:t + 1], -1.0 / 1024, None, ALU.mult), a0)
        v = dve.do(lambda e: e.tensor_scalar(AV[:, t, :], AV[:, t, :], mu2[:, t:t + 1], None, ALU.add), v)
        jk_tok[0] = act.do(lambda e: e.activation(JK_[0][:, :], AV[:, t, :], ACT.Square, accum_out=vs2[:, t:t + 1]),
                           v, jk_tok[0])
        if t == 1:
            p = inv_root(rv2, vs2, 2, 1024, LN_EPS, jk_tok[0])
            for tt in range(2):
                t_vn[tt] = dve.do(lambda e: e.tensor_scalar(AV[:, tt, :], AV[:, tt, :], rv2[:, tt:tt + 1], None, ALU.mult), p)
        return [a0]

    run(U["ab"][0], nm3["got"], ev_av, [nm3["stats"]], nm3["feed"], [nm3["stats"]])
    t_mx = {}

    def mixing():
        for t in range(2):
            for hf in range(2):
                bank, fr = side.take()
                for q in range(4):
                    g = 4 * hf + q
                    o = PS[:, bank, q * 128:(q + 1) * 128]
                    tk = pe.do(lambda e, o=o, g=g: e.matmul(o, WS[:, g, :], AV[:, t, g * 128:(g + 1) * 128],
                                                            start=True, stop=True), fr, t_wm, t_vn[t], sig=(q == 3))
                d = AV[:, t, 512 * hf:512 * hf + 512].rearrange("p (g c) -> p g c", g=4)
                s = PS[:, bank, :].rearrange("p (g c) -> p g c", g=4)
                t_mx[t] = dve.do(lambda e: e.tensor_tensor(d, s, bcast(par("bs", 4 * hf, 4), 2, 128), ALU.add), tk)
                side.done(bank, [t_mx[t]])
                yield

    evg = to_sb(lambda t: GC[:, t, :], nm3)
    mxg = mixing()
    run(U["ab"][1], nm3["got"], evg, [mxg])
    t_z = [None, None]

    def ev_z(t, b, tok):
        t_z[t] = dve.do(lambda e: e.scalar_tensor_tensor(out=GC[:, t, :], in0=flat2(b), scalar=rr[:, t:t + 1],
                                                         in1=GC[:, t, :], op0=ALU.mult, op1=ALU.mult),
                        tok, evg.toks[t])
        return [t_z[t]]
    run(U["ab"][2], nm3["got"], ev_z)
    finish(mxg)
    t_zT = {}

    def z_turn():
        for c in range(0, 8, 2):
            bank, fr = side.take()
            for q in range(2):
                for t in range(2):
                    o = PS[:, bank, q * 256 + t * 128:q * 256 + t * 128 + 128]
                    s = GC[:, t, (c + q) * 128:(c + q + 1) * 128]
                    tk = pe.do(lambda e, o=o, s=s: e.transpose(o, s, ID[:, :]), fr, t_z[t], sig=(q == 1 and t == 1))
            a = act.do(lambda e: e.activation(ZT[:, c:c + 2, 2:258], PS[:, bank, :].rearrange("p (a b) -> p a b", a=2),
                                              ACT.Copy), tk)
            side.done(bank, [a])
            t_zT[c] = t_zT[c + 1] = a
            yield
    zg = z_turn()
    evb = to_sb(lambda t: GB[:, t, :], nm3)
    run(U["ab"][3], nm3["got"], evb, [zg])
    finish(zg)
    bk_ = []

    def conv_side():
        prev = None
        for c in range(0, 8, 2):
            bank, fr = side.take()
            for q in range(2):
                for t in range(2):
                    o = PS[:, bank, q * 256 + t * 128:q * 256 + t * 128 + 128]
                    s = GB[:, t, (c + q) * 128:(c + q + 1) * 128]
                    tk = pe.do(lambda e, o=o, s=s: e.transpose(o, s, ID[:, :]), fr, evb.toks[t], sig=(q == 1 and t == 1))
            for q in range(2):
                k = c + q
                cw = [par("conv", 8 * tap + k, 1) for tap in range(3)]
                v = dve.do(lambda e: e.tensor_scalar(CV[0][:, :], ZT[:, k, 0:256], cw[0], None, ALU.mult), t_zT[k], t_zz, prev)
                v = dve.do(lambda e: e.scalar_tensor_tensor(out=CV[1][:, :], in0=ZT[:, k, 1:257], scalar=cw[1],
                                                            in1=CV[0][:, :], op0=ALU.mult, op1=ALU.add), v)
                v = dve.do(lambda e: e.scalar_tensor_tensor(out=CV[2][:, :], in0=ZT[:, k, 2:258], scalar=cw[2],
                                                            in1=CV[1][:, :], op0=ALU.mult, op1=ALU.add), v)
                v = dve.do(lambda e: e.tensor_tensor(BO[:, q, :], CV[2][:, :], PS[:, bank, q * 256:q * 256 + 256],
                                                     ALU.mult), v, tk)
                prev = v
            side.done(bank, [v])
            pair, pf = take_pair()
            kt, ks = kslot(2 * pair)
            a = act.do(lambda e: e.activation(kt[:, ks:ks + 2, 0, :], BO[:, :, :], ACT.Copy), v, pf)
            prev = dve.do(lambda e: e.tensor_tensor(kt[:, ks:ks + 2, 1, :], BO[:, :, :],
                                                    kt[:, ks:ks + 2, 0, :].bitcast(F32), ALU.subtract), a, pf)
            for q in range(2):
                bk_.append((2 * pair + q, [a, prev]))
            yield
    cg = conv_side()
    t_ao = [None, None]

    def ev_au(t, b, tok):
        a = act.do(lambda e: e.activation(GC[:, t, :], flat2(b), ACT.Gelu_apprx_tanh, scale=rr[:, t:t + 1]),
                   tok, t_zT[7])
        t_ao[t] = dve.do(lambda e: e.tensor_tensor(GC[:, t, :], GC[:, t, :], AV[:, t, :], ALU.mult), a, t_mx[t])
        return [a]
    tl = run(U["ab"][4], nm3["got"], ev_au, [cg])
    finish(cg)
    give(nm3["got"], tl)
    akf = feed(lambda c, t: GC[:, t, c * 128:(c + 1) * 128], None, bk_, [t_ao] * 8)

    GP = sb([128, D], stack=ph, name="GP")
    acc_tok = {}

    def post(name, idx, dst_g):
        return load(dst_g[:, :], inp[name][idx:idx + 1, :].partition_broadcast(128).rearrange("p a c -> p (a c)"))

    def post_state():
        return dict(part=small(4), ss=small(2), r=small(2))

    def ev_post(c, psn, g, tg, add):
        def evac(t, b, tok):
            d = ACC[:, t, c * 1024:(c + 1) * 1024]
            if add:
                v0 = dve.do(lambda e: e.tensor_tensor(d, flat2(b), d, ALU.add), tok, acc_tok.get((t, c)))
            else:
                v0 = dve.do(lambda e: e.tensor_copy(d, flat2(b)), tok, acc_tok.get((t, c)))
            psn[("v", t, c)] = v0
            psn[("j", t, c)] = jk_tok[0] = act.do(
                lambda e: e.activation(JK_[0][:, :], d, ACT.Square, accum_out=psn["part"][:, 2 * c + t:2 * c + t + 1]),
                v0, jk_tok[0])
            if c == 0:
                psn["gain"](t, c)
            return [v0]

        def gain(t, c):
            d = ACC[:, t, c * 1024:(c + 1) * 1024]
            acc_tok[(t, c)] = dve.do(lambda e: e.tensor_tensor(d, d, g[:, c * 1024:(c + 1) * 1024], ALU.mult),
                                     psn[("v", t, c)], tg, psn[("j", t, c)])
        psn["gain"] = gain
        return evac

    def post_add(psn):
        psn["gain"](0, 1)
        a = add_small(psn["ss"], psn["part"][:, 0:2], psn["part"][:, 2:4], psn[("j", 1, 1)], psn[("j", 0, 1)],
                      psn[("j", 1, 0)], psn[("j", 0, 0)])
        p = inv_root(psn["r"], psn["ss"], 2, D, EPS, a)
        psn["gain"](1, 1)
        for c in range(4):
            for t in range(2):
                s, d = ACC[:, t, c * 512:(c + 1) * 512], XR[:, t, c * 512:(c + 1) * 512]
                xr_tok[(t, c)] = dve.do(lambda e: e.scalar_tensor_tensor(out=d, in0=s, scalar=psn["r"][:, t:t + 1], in1=d,
                                                                         op0=ALU.mult, op1=ALU.add),
                                        p, acc_tok[(t, c // 2)], xr_tok[(t, c)])
        for c in range(2):
            for t in range(2):
                acc_tok[(t, c)] = xr_tok[(t, 2 * c + 1)]

    tg = post("norm_mix_post", 0, GP)
    psn = post_state()
    for c in range(2):
        tl = run(U["oab"][c], bk_, ev_post(c, psn, GP, tg, False), feeder=akf)
    give(bk_, tl)
    post_add(psn)

    def ffn2(nm, layer):
        ups, dns, order = F2[layer]
        H = [sb([128, 2, 1024], stack=ph, name="HS") for _ in range(2)]
        RL = sb([128, 1024], stack=ph, name="RL")
        G = sb([128, D], stack=ph, name="GP")
        tgg = post("norm_mlp_post", layer, G)
        psn = post_state()
        rd = [None, None]
        rl_tok = [None]
        hid2 = {}
        pend = []
        for kind, b in order:
            if kind == "up":
                Hb = H[b % 2]
                th = [None, None]

                def evac(t, bk, tok):
                    a = act.do(lambda e: e.activation(RL[:, :], flat2(bk), ACT.Relu, scale=nm["r"][:, t:t + 1]),
                               tok, nm["tr"], rl_tok[0])
                    rl_tok[0] = th[t] = dve.do(lambda e: e.tensor_tensor(Hb[:, t, :], RL[:, :], RL[:, :], ALU.mult),
                                               a, rd[b % 2])
                    return [a]
                if b:
                    run(ups[b], nm["got"], evac, pend)
                else:
                    run(ups[b], nm["got"], evac, [nm["stats"]], nm["feed"], [nm["stats"]])
                for g in pend:
                    finish(g)
                if b == len(ups) - 1:
                    give(nm["got"], pe.last())
                got = hid2.setdefault(b, [])

                def g_(Hb=Hb, th=th, got=got, b=b):
                    yield
                    yield
                    yield from feed(lambda c, t: Hb[:, t, c * 128:(c + 1) * 128], None, got, [th] * 8)
                    rd[b % 2] = pe.last()
                pend = [g_()]
                if b == 0:
                    pass
            else:
                final = b == len(ups) - 1
                if final:
                    for g in pend:
                        finish(g)
                    pend = []
                for c in range(2):
                    if final:
                        ev = ev_post(c, psn, G, tgg, True)
                    else:
                        def ev(t, bk, tok, c=c):
                            d = ACC[:, t, c * 1024:(c + 1) * 1024]
                            if b == 0:
                                v = dve.do(lambda e: e.tensor_copy(d, flat2(bk)), tok, acc_tok.get((t, c)))
                            else:
                                v = dve.do(lambda e: e.tensor_tensor(d, flat2(bk), d, ALU.add), tok, acc_tok.get((t, c)))
                            acc_tok[(t, c)] = v
                            return [v]
                    tl = run(dns[b][c], hid2[b], ev, pend)
                for g in pend:
                    finish(g)
                pend = []
                give(hid2[b], tl)
        post_add(psn)

    nm4 = new_norm("mpre0")
    phase()
    JK_[0] = sb([128, 1024], stack=ph, name="JK")
    ffn2(nm4, 0)

    nm5 = new_norm("pre1")
    phase()
    JK_[0] = sb([128, 1024], stack=ph, name="JK")
    q2 = sb([128, 8, 256], stack=ph, name="q2T")
    k2 = sb([128, 8, 256], stack=ph, name="k2T")
    v2_ = [ACC[:, h, :].rearrange("p (t c) -> p t c", t=2) for h in range(2)]
    TKS = [sb([128, 2, 1024], stack=ph, name="TK") for _ in range(2)]
    M1, M2 = JK_[0][:, 0:512], JK_[0][:, 512:1024]
    CS = sb([128, 2, 2, 64], stack=ph, name="CS")
    DM = sb([128, 384], stack=ph, name="DM")
    B2 = attn_buffers(ph, ph, AB[0]["stats"])
    OS = sb([128, 2, 1024], stack=ph, name="OS")
    t_cs = load(CS[:, :, :, :].rearrange("p a b c -> p (a b c)"), inp["rope"])
    t_dm = load(DM[:, :], inp["dilmask"])
    t_rc = [None]

    def rope_scale():
        for t in range(2):
            c_ = CS[:, t, :, :].rearrange("p a b -> p (a b)")
            t_rc[0] = dve.do(lambda e: e.tensor_scalar(c_, c_, nm5["r"][:, t:t + 1], None, ALU.mult), t_cs, nm5["tr"])
        yield
    tk_free = [None, None]
    m_free = [None]

    def ev_rope(toks, which):
        TK = TKS[which]

        def evac(t, b, tok):
            ps4 = flat2(b).rearrange("p (h s d) -> p h s d", h=8, s=2)
            o4 = TK[:, t, :].rearrange("p (h s d) -> p h s d", h=8, s=2)
            m1, m2 = M1[:, :].rearrange("p (h d) -> p h d", h=8), M2[:, :].rearrange("p (h d) -> p h d", h=8)
            cs, sn = bcast(CS[:, t, 0, :], 1, 8), bcast(CS[:, t, 1, :], 1, 8)
            a_, b_ = ps4[:, :, 0, :], ps4[:, :, 1, :]
            dve.do(lambda e: e.tensor_tensor(o4[:, :, 0, :], a_, cs, ALU.mult), tok, t_rc[0], tk_free[which], jk_tok[0])
            va = dve.do(lambda e: e.tensor_tensor(m1, b_, sn, ALU.mult), m_free[0])
            p = pool.do(lambda e: e.tensor_tensor(o4[:, :, 0, :], o4[:, :, 0, :], m1, ALU.subtract), va)
            dve.do(lambda e: e.tensor_tensor(o4[:, :, 1, :], b_, cs, ALU.mult))
            vb = dve.do(lambda e: e.tensor_tensor(m2, a_, sn, ALU.mult))
            p = pool.do(lambda e: e.tensor_tensor(o4[:, :, 1, :], o4[:, :, 1, :], m2, ALU.add), vb)
            toks[t] = p
            m_free[0] = p
            return [vb]
        return evac

    tT = [{}, {}]

    def turn8(dst, which, toks, busy):
        for c in range(0, 8, 2):
            a = turn(lambda cc, t: TKS[which][:, t, cc * 128:(cc + 1) * 128], dst, c, None, list(toks), busy)
            tT[which][c] = tT[which][c + 1] = a
            tk_free[which] = pe.last()
            yield
    os_free = [None]
    oks = [[], []]
    t_os = {}

    def late(g, n):
        for _ in range(n):
            yield
        yield from g

    def attn2(hf, tv, vd):
        tr_now = [dict(tT[0]), dict(tT[1])]
        for g in range(2):
            def write(t, h0, per, src, r, tk, trr):
                c0 = (4 * g + h0) * 128
                d = OS[:, t, c0:c0 + per * 128].rearrange("p (h d) -> p h d", h=per)
                t_os[(hf, t, 4 * g + h0)] = dve.do(lambda e: e.tensor_tensor(d, src, r, ALU.mult), tk, trr, os_free[0])
                return t_os[(hf, t, 4 * g + h0)]
            yield from attn_group(g, lambda h: q2[:, 4 * g + h, :], lambda h: k2[:, 4 * g + h, :],
                                  lambda h, t: vd[:, t, (4 * g + h) * 128:(4 * g + h + 1) * 128], 128,
                                  128.0 ** -0.5, lambda h: DM[:, :], t_dm, None, write, B2,
                                  [[tr_now[0][4 * g + h], tr_now[1][4 * g + h], tv] for h in range(4)])
            yield from feed(lambda c, t: OS[:, t, (4 * g + c) * 128:(4 * g + c + 1) * 128], None, oks[hf],
                            [[t_os[(hf, 0, 4 * g + 2 * (c // 2))], t_os[(hf, 1, 4 * g + 2 * (c // 2))]] for c in range(4)])
        os_free[0] = pe.last()

    main.banks, main.at = [0, 2], 0
    side.free[4] = list(main.free[4])
    side.free[5] = list(main.free[4])
    side.banks = [4, 5, 6, 7]
    old = None
    for hf in range(2):
        tq, tkk = [None, None], [None, None]
        if hf:
            run(U["qkv"][hf][0], nm5["got"], ev_rope(tq, 0), [old])
        else:
            run(U["qkv"][hf][0], nm5["got"], ev_rope(tq, 0), [nm5["stats"]], nm5["feed"], [nm5["stats"], rope_scale()])
        gq = turn8(q2, 0, tq, None)
        run(U["qkv"][hf][1], nm5["got"], ev_rope(tkk, 1), [old] if hf else [late(gq, 2)])
        if hf:
            finish(old)
        finish(gq)
        gk = turn8(k2, 1, tkk, None)
        vd = TKS[1] if hf else v2_[0]
        ev = to_sb(lambda t: vd[:, t, :], nm5)
        act.wait(list(acc_tok.values()))
        tl = run(U["qkv"][hf][2], nm5["got"], ev, [late(gk, 2)], ends=[gk])
        old = attn2(hf, ev.toks, vd)
    give(nm5["got"], tl)
    gate = all_done()
    for t in range(2):
        for c in range(2):
            acc_tok[(t, c)] = gate
    for c in range(2):
        def ev(t, bk, tok, c=c):
            d = ACC[:, t, c * 1024:(c + 1) * 1024]
            v = dve.do(lambda e: e.tensor_copy(d, flat2(bk)), tok, acc_tok[(t, c)])
            acc_tok[(t, c)] = v
            return [v]
        tl = run(U["wo"][0][c], oks[0], ev, [old, old])
    give(oks[0], tl)
    finish(old)
    main.banks, main.at = [0, 2, 4], 0
    main.free[4] = side.free[4] + side.free[5]
    side.banks = [6, 7]
    phase()
    JK_[0] = sb([128, 1024], stack=ph, name="JK")
    GP2 = sb([128, D], stack=ph, name="GP")
    tg = post("norm_mix_post", 1, GP2)
    psn = post_state()
    for c in range(2):
        tl = run(U["wo"][1][c], oks[1], ev_post(c, psn, GP2, tg, True))
    give(oks[1], tl)
    post_add(psn)
    nm6 = new_norm("mpre1")
    ffn2(nm6, 1)

    s_out = sem("out_written")
    for c in range(4):
        for t in range(2):
            sp.wait(xr_tok[(t, c)])
            s, d = XR[:, t, c * 512:(c + 1) * 512], out[t * 128:(t + 1) * 128, c * 512:(c + 1) * 512]
            sp.do(lambda e, s=s, d=d: e.dma_start(d, s).then_inc(s_out, 16), sig=False)
    sp.wait((s_out, 128), (s_w, 16))
    assert state["split"] == len(steps) and state["dma"] == len(dmas)


def _buckets():
    dist = np.arange(128)
    nf = np.maximum(dist, 1).astype(np.float32)
    large = 16 + (np.log(nf / 16) / np.log(128 / 16) * 16).astype(np.int32)
    return np.where(dist < 16, dist, np.minimum(large, 31)).astype(np.int32)


def constants():
    c = {"ident": np.eye(128, dtype=np.float32)}
    onehot = np.zeros((33, 383), np.float32)
    bk = _buckets()
    for x in range(383):
        dist = 255 - x
        if 0 <= dist < 128:
            onehot[bk[dist], x] = 1.0
        else:
            onehot[32, x] = NEG
    c["onehot"] = onehot
    c["tau"] = np.ascontiguousarray(np.broadcast_to(np.arange(256, dtype=np.float32), (128, 256)))
    c["causal"] = np.triu(np.ones((128, 128), np.float32))
    half = 64
    inv = (np.float32(10000.0) ** (-np.arange(half, dtype=np.float32) * np.float32(2.0) / np.float32(128))).astype(np.float32)
    angle = np.arange(256, dtype=np.float32)[:, None] * inv[None, :]
    cs = np.stack([np.cos(angle.astype(np.float64)), np.sin(angle.astype(np.float64))], 1).astype(np.float32)
    c["rope"] = np.ascontiguousarray(cs.reshape(2, 128, 2, half).transpose(1, 0, 2, 3).reshape(128, 256))
    t = np.arange(256)[:, None]
    j = np.arange(256)[None, :]
    d = t - j
    count = ((d >= 0) & (d <= 128)).astype(int) + ((d >= 0) & (d % 4 == 0)) + ((d >= 0) & (d % 16 == 0))
    lc = np.where(count > 0, np.log(np.maximum(count, 1)), NEG).astype(np.float32)
    c["dilmask"] = np.ascontiguousarray(np.concatenate([lc[:128, :128], lc[128:, :]], 1))
    return c


def kernel(**inputs):
    import concourse.bacc as _bacc
    from concourse.bass_utils import run_bass_kernel_spmd as _run

    f = {k: np.asarray(v) for k, v in inputs.items()}
    feat = lambda a, n: a.reshape(n, 128).T
    states = lambda a: a.reshape(32, 128).T
    rep = lambda a: np.broadcast_to(a, (128, a.shape[-1]))
    p = np.zeros((128, NPAR), np.float32)

    def put(name, a):
        p[:, COLS[name][0]:COLS[name][1]] = a
    put("ln1", feat(f["ln1_g"][0], 16))
    put("ln2", feat(f["ln2_g"][0], 16))
    for l in range(2):
        put(f"pre{l}", feat(f["norm_mix_pre_2"][l], 16))
        put(f"mpre{l}", feat(f["norm_mlp_pre_2"][l], 16))
    put("attn_g", feat(f["attn_out_g"][0], 8))
    put("ssm_g", feat(f["ssm_out_g"][0], 8))
    put("qg", np.concatenate([f["q_norm_g"][0]] * 2)[:, None])
    put("kg", np.concatenate([f["k_norm_g"][0]] * 2)[:, None])
    put("d", feat(f["ssm_d"][0], 8))
    put("a_re", states(f["ssm_a_re"][0]))
    put("a_im", states(f["ssm_a_im"][0]))
    put("ldt", states(np.repeat(f["ssm_log_dt"][0], 64)))
    put("conv", f["conv_w_2"][0].reshape(3, 8, 128).transpose(2, 0, 1).reshape(128, 24))
    put("bs", f["b_spatial_2"][0].T)
    put("sinks", rep(f["attn_sinks"][0]))

    b = np.stack([f["ssm_b_re"][0], f["ssm_b_im"][0]]).reshape(2, 32, 128, 16).transpose(0, 2, 1, 3).reshape(2, 128, 512)
    cc = np.zeros((2, 64, 2, 32, 2, 16), np.float32)
    for i, name in enumerate(("ssm_c_re", "ssm_c_im")):
        a = f[name][0].reshape(32, 2, 16, 64)
        for g in range(2):
            cc[g, :, i, :, g, :] = a[:, g].transpose(2, 0, 1)
    arrays = {
        "x": f["x"][0], "w_in": f["w_in"][0], "w_glu": f["w_glu"][0], "w_out": f["w_out"][0],
        "w_ff_gate": f["w_ff_gate"][0], "w_ff_up": f["w_ff_up"][0], "w_ff_down": f["w_ff_down"][0],
        "w_in_ab": f["w_in_ab_2"][0], "w_out_ab": f["w_out_ab_2"][0], "w_qkv": f["w_qkv_2"][0], "w_o": f["w_o_2"][0],
        "w_up": f["w_up_2"], "w_down": f["w_down_2"], "rel_bias": f["rel_bias"],
        "norm_mix_post": f["norm_mix_post_2"], "norm_mlp_post": f["norm_mlp_post_2"],
        "params": p, "ssm_b": b, "ssm_c": cc.reshape(128, 2048),
        "w_spatial": f["w_spatial_2"][0].transpose(2, 0, 1).reshape(128, 1024),
    }
    arrays.update(constants())
    nc = _bacc.Bacc("TRN2", target_bir_lowering=False, num_devices=1)
    feeds, inp = {}, {}
    for name, a in arrays.items():
        a = np.ascontiguousarray(a)
        feeds[f"in_{name}"] = a
        inp[name] = nc.dram_tensor(f"in_{name}", a.shape, mybir.dt.from_np(a.dtype), kind="ExternalInput").ap()
    out = nc.dram_tensor("out_x", (256, D), F32, kind="ExternalOutput").ap()
    scratch = nc.dram_tensor("bias_rows", (16, 128, 384), F32, kind="Internal").ap()
    program(nc, inp, out, scratch)
    r = _run(nc, [feeds], core_ids=[0])
    return r.results[0]["out_x"].reshape(1, 256, D)
```
